# Optimizing a Trainium2 kernel written in Bass

```python
import jax, jax.numpy as jnp
from jax import lax
import numpy as np

D_MODEL = 1024
BATCH = 1
SEQ = 256
DEPTH = 2

CHUNK = 64
HEAD_DIM = 64
A_HEADS = 8
A_WIDTH = A_HEADS * HEAD_DIM
A_LEFT_CHUNKS = 8
A_BAND = (A_LEFT_CHUNKS + 1) * CHUNK
REL_CLIP = 256
POOL_WINDOWS = (2, 4, 8, 16)
POOL_GROUPS = 4
POOL_GROUP_DIM = 128
B_WIDTH = POOL_GROUPS * POOL_GROUP_DIM
C_HEADS = 4
C_QK_WIDTH = C_HEADS * 2 * HEAD_DIM
C_V_DIM = 2 * HEAD_DIM
C_WIDTH = C_HEADS * C_V_DIM
Q_BLOCK = 128
ROPE_THETA = 500000.0
ROPE_DIM = HEAD_DIM // 4
N_BRANCH = 3
IN_SIZES = [A_WIDTH] * 3 + [B_WIDTH] + [C_QK_WIDTH] * 2 + [C_WIDTH] + [D_MODEL] * N_BRANCH
D_IN = sum(IN_SIZES)
N_EXPERTS = 64
TOP_K = 8
N_GROUPS = 8
TOPK_GROUPS = 4
EXPERT_DIM = 256
ROUTED_SCALE = 2.5
DISPATCH_BLOCK = 128
DN_ALPHA = (2 * DEPTH) ** 0.25
DN_BETA = (8 * DEPTH) ** -0.25
LN_EPS = 1e-5
RMS_EPS = 1e-5

kernel_name = "hybrid_chunk_causal_moe_trunk"

def layer_norm(x, g, b):
    x32 = x.astype(jnp.float32)
    mu = jnp.mean(x32, axis=-1, keepdims=True)
    var = jnp.mean(jnp.square(x32 - mu), axis=-1, keepdims=True)
    return ((x32 - mu) * lax.rsqrt(var + LN_EPS)).astype(x.dtype) * g + b

def rope_tables(seq, dtype):
    inv = ROPE_THETA ** (-jnp.arange(0, ROPE_DIM, 2, dtype=jnp.float32) / ROPE_DIM)
    ang = jnp.arange(seq, dtype=jnp.float32)[:, None] * inv[None, :]
    return jnp.cos(ang).astype(dtype), jnp.sin(ang).astype(dtype)

def apply_partial_rope(x, cos, sin):
    half = ROPE_DIM // 2
    x1, x2, rest = x[..., :half], x[..., half:ROPE_DIM], x[..., ROPE_DIM:]
    c = cos[:, None, None, :]
    s = sin[:, None, None, :]
    return jnp.concatenate([x1 * c - x2 * s, x2 * c + x1 * s, rest], axis=-1)

def chunked_relpos_attention(q, k, v, rel_bias):
    B, S = q.shape[:2]
    nc = S // CHUNK
    shp = (B, nc, CHUNK, A_HEADS, HEAD_DIM)
    qc = q.reshape(shp)
    pad = ((0, 0), (A_LEFT_CHUNKS, 0), (0, 0), (0, 0), (0, 0))
    kp = jnp.pad(k.reshape(shp), pad)
    vp = jnp.pad(v.reshape(shp), pad)
    band_shape = (B, nc, A_BAND, A_HEADS, HEAD_DIM)
    kb = jnp.stack([kp[:, j:j + nc] for j in range(A_LEFT_CHUNKS + 1)], axis=2).reshape(band_shape)
    vb = jnp.stack([vp[:, j:j + nc] for j in range(A_LEFT_CHUNKS + 1)], axis=2).reshape(band_shape)
    s = jnp.einsum('bcqhd,bckhd->bhcqk', qc, kb).astype(jnp.float32) * (HEAD_DIM ** -0.5)
    qpos = A_LEFT_CHUNKS * CHUNK + jnp.arange(CHUNK)
    kpos = jnp.arange(A_BAND)
    rel = jnp.clip(qpos[:, None] - kpos[None, :], -REL_CLIP, REL_CLIP) + REL_CLIP
    bias = rel_bias[:, rel].astype(jnp.float32)
    valid = (jnp.arange(nc)[:, None] + kpos[None, :] // CHUNK) >= A_LEFT_CHUNKS
    s = jnp.where(valid[None, None, :, None, :], s + bias[None, :, None], -jnp.inf)
    p = jax.nn.softmax(s, axis=-1).astype(v.dtype)
    o = jnp.einsum('bhcqk,bckhd->bcqhd', p, vb)
    return o.reshape(B, S, A_WIDTH)

def multiscale_pool_mixer(u, pool_w, pool_scale):
    B, S, _ = u.shape
    ug = u.reshape(B, S, POOL_GROUPS, POOL_GROUP_DIM).astype(jnp.float32)
    csp = jnp.pad(jnp.cumsum(ug, axis=1), ((0, 0), (1, 0), (0, 0), (0, 0)))
    t = jnp.arange(S)
    pooled = []
    for g, w in enumerate(POOL_WINDOWS):
        hi = csp[:, 1:, g]
        lo = jnp.pad(csp[:, :S + 1 - w, g], ((0, 0), (w - 1, 0), (0, 0)))
        cnt = jnp.minimum(t + 1, w).astype(jnp.float32)[None, :, None]
        pooled.append((hi - lo) / cnt)
    mixed = (jnp.stack(pooled, axis=2) - ug).astype(u.dtype)
    y = jnp.einsum('bsgc,gcd->bsgd', mixed, pool_w).reshape(B, S, B_WIDTH)
    return y * pool_scale

def differential_attention(q, k, v, lam, lambda_init, subln_g, cos, sin):
    B, S = q.shape[:2]
    q = apply_partial_rope(q, cos, sin) * (HEAD_DIM ** -0.5)
    k = apply_partial_rope(k, cos, sin)
    nqb = S // Q_BLOCK
    qb = jnp.moveaxis(q.reshape(B, nqb, Q_BLOCK, C_HEADS, 2, HEAD_DIM), 1, 0)
    k_chunk = jnp.arange(S) // CHUNK

    def one_block(args):
        qblk, i = args
        s = jnp.einsum('bqhcd,bkhcd->bhcqk', qblk, k).astype(jnp.float32)
        q_chunk = (i * Q_BLOCK + jnp.arange(Q_BLOCK)) // CHUNK
        mask = k_chunk[None, :] <= q_chunk[:, None]
        p = jax.nn.softmax(jnp.where(mask, s, -jnp.inf), axis=-1)
        attn = (p[:, :, 0] - lam * p[:, :, 1]).astype(v.dtype)
        return jnp.einsum('bhqk,bkhe->bqhe', attn, v)

    o = lax.map(one_block, (qb, jnp.arange(nqb)))
    o = jnp.moveaxis(o, 0, 1).reshape(B, S, C_HEADS, C_V_DIM)
    o32 = o.astype(jnp.float32)
    o = (o32 * lax.rsqrt(jnp.mean(o32 * o32, axis=-1, keepdims=True) + RMS_EPS)).astype(v.dtype) * subln_g
    return (o * (1.0 - lambda_init)).reshape(B, S, C_WIDTH)

def hybrid_mixer(x, layer_idx, w_in, rel_bias, pool_w, pool_scale, lambda_q1, lambda_k1,
                 lambda_q2, lambda_k2, subln_g, w_branch_a, w_branch_b, w_branch_c, w_out, cos, sin):
    B, S, _ = x.shape
    z = x @ w_in
    bounds = [int(v) for v in np.cumsum(IN_SIZES)[:-1]]
    qa, ka, va, ub, qc, kc, vc, ga, gb, gc = jnp.split(z, bounds, axis=-1)
    a_shape = (B, S, A_HEADS, HEAD_DIM)
    ya = chunked_relpos_attention(qa.reshape(a_shape), ka.reshape(a_shape), va.reshape(a_shape), rel_bias)
    yb = multiscale_pool_mixer(ub, pool_w, pool_scale)
    lambda_init = 0.8 - 0.6 * float(np.exp(-0.3 * layer_idx))
    lam = (jnp.exp(jnp.sum(lambda_q1.astype(jnp.float32) * lambda_k1.astype(jnp.float32)))
           - jnp.exp(jnp.sum(lambda_q2.astype(jnp.float32) * lambda_k2.astype(jnp.float32)))
           + lambda_init)
    c_shape = (B, S, C_HEADS, 2, HEAD_DIM)
    yc = differential_attention(qc.reshape(c_shape), kc.reshape(c_shape),
                                vc.reshape(B, S, C_HEADS, C_V_DIM), lam, lambda_init, subln_g, cos, sin)
    merged = (jax.nn.sigmoid(ga) * (ya @ w_branch_a)
              + jax.nn.sigmoid(gb) * (yb @ w_branch_b)
              + jax.nn.sigmoid(gc) * (yc @ w_branch_c))
    return merged @ w_out

def route(x_flat, router_w, router_bias):
    n = x_flat.shape[0]
    scores = jax.nn.sigmoid((x_flat @ router_w).astype(jnp.float32))
    choice = scores + router_bias.astype(jnp.float32)
    grp = choice.reshape(n, N_GROUPS, N_EXPERTS // N_GROUPS)
    grp_score = jnp.sum(lax.top_k(grp, 2)[0], axis=-1)
    _, top_groups = lax.top_k(grp_score, TOPK_GROUPS)
    gmask = jnp.sum(jax.nn.one_hot(top_groups, N_GROUPS), axis=1) > 0
    emask = jnp.repeat(gmask, N_EXPERTS // N_GROUPS, axis=1)
    _, idx = lax.top_k(jnp.where(emask, choice, -jnp.inf), TOP_K)
    w = jnp.take_along_axis(scores, idx, axis=-1)
    w = w / jnp.sum(w, axis=-1, keepdims=True) * ROUTED_SCALE
    return idx, w.astype(x_flat.dtype)

def routed_experts(x_flat, idx, wts, w_gate_up, w_down):
    n, d = x_flat.shape
    nk = n * TOP_K
    e = idx.reshape(nk)
    tok = jnp.arange(nk, dtype=jnp.int32) // TOP_K
    gate = wts.reshape(nk)
    order = jnp.argsort(e)
    e_s, tok_s, gate_s = e[order], tok[order], gate[order]
    counts = jnp.zeros((N_EXPERTS,), jnp.int32).at[e].add(1)
    padded = (counts + DISPATCH_BLOCK - 1) // DISPATCH_BLOCK * DISPATCH_BLOCK
    start = jnp.cumsum(counts) - counts
    pend = jnp.cumsum(padded)
    pstart = pend - padded
    dest = pstart[e_s] + (jnp.arange(nk, dtype=jnp.int32) - start[e_s])
    nb = (nk + DISPATCH_BLOCK - 1) // DISPATCH_BLOCK + N_EXPERTS
    rows = nb * DISPATCH_BLOCK
    row_tok = jnp.full((rows,), n, jnp.int32).at[dest].set(tok_s)
    row_gate = jnp.zeros((rows,), gate.dtype).at[dest].set(gate_s)
    blk_expert = jnp.minimum(
        jnp.searchsorted(pend, jnp.arange(nb, dtype=jnp.int32) * DISPATCH_BLOCK, side='right'),
        N_EXPERTS - 1)
    x_pad = jnp.concatenate([x_flat, jnp.zeros((1, d), x_flat.dtype)], axis=0)

    def one_block(args):
        t, g, ex = args
        h = x_pad[t] @ w_gate_up[ex]
        h = jax.nn.silu(h[:, :EXPERT_DIM]) * h[:, EXPERT_DIM:]
        return (h @ w_down[ex]) * g[:, None]

    y = lax.map(one_block, (row_tok.reshape(nb, DISPATCH_BLOCK),
                            row_gate.reshape(nb, DISPATCH_BLOCK), blk_expert))
    out = jnp.zeros((n + 1, d), y.dtype).at[row_tok].add(y.reshape(rows, d))
    return out[:n]

def shared_expert(x_flat, w_gate_up, w_down):
    h = x_flat @ w_gate_up
    return (jax.nn.silu(h[:, :EXPERT_DIM]) * h[:, EXPERT_DIM:]) @ w_down

def setup_inputs(seed: int = 0) -> dict:
    key = jax.random.key(seed)
    ks = jax.random.split(key, 24)
    L, D, E, F = DEPTH, D_MODEL, N_EXPERTS, EXPERT_DIM

    def nrm(k, shape, scale):
        return jax.random.normal(k, shape, jnp.float32) * scale

    return {
        "x": nrm(ks[0], (BATCH, SEQ, D), 1.0),
        "w_in": nrm(ks[1], (L, D, D_IN), D ** -0.5),
        "rel_bias": nrm(ks[2], (L, A_HEADS, 2 * REL_CLIP + 1), 0.2),
        "pool_w": nrm(ks[3], (L, POOL_GROUPS, POOL_GROUP_DIM, POOL_GROUP_DIM), POOL_GROUP_DIM ** -0.5),
        "pool_scale": 1.0 + nrm(ks[4], (L, B_WIDTH), 0.05),
        "lambda_q1": nrm(ks[5], (L, HEAD_DIM), 0.1),
        "lambda_k1": nrm(ks[6], (L, HEAD_DIM), 0.1),
        "lambda_q2": nrm(ks[7], (L, HEAD_DIM), 0.1),
        "lambda_k2": nrm(ks[8], (L, HEAD_DIM), 0.1),
        "subln_g": 1.0 + nrm(ks[9], (L, C_V_DIM), 0.05),
        "w_branch_a": nrm(ks[10], (L, A_WIDTH, D), A_WIDTH ** -0.5),
        "w_branch_b": nrm(ks[11], (L, B_WIDTH, D), B_WIDTH ** -0.5),
        "w_branch_c": nrm(ks[12], (L, C_WIDTH, D), C_WIDTH ** -0.5),
        "w_out": nrm(ks[13], (L, D, D), D ** -0.5 * DN_BETA),
        "ln1_g": 1.0 + nrm(ks[14], (L, D), 0.05),
        "ln1_b": nrm(ks[15], (L, D), 0.02),
        "router_w": nrm(ks[16], (L, D, E), D ** -0.5),
        "router_bias": nrm(ks[17], (L, E), 0.01),
        "expert_w_gate_up": nrm(ks[18], (L, E, D, 2 * F), D ** -0.5),
        "expert_w_down": nrm(ks[19], (L, E, F, D), F ** -0.5 * DN_BETA),
        "shared_w_gate_up": nrm(ks[20], (L, D, 2 * F), D ** -0.5),
        "shared_w_down": nrm(ks[21], (L, F, D), F ** -0.5 * DN_BETA),
        "ln2_g": 1.0 + nrm(ks[22], (L, D), 0.05),
        "ln2_b": nrm(ks[23], (L, D), 0.02),
    }

def reference(x, w_in, rel_bias, pool_w, pool_scale, lambda_q1, lambda_k1, lambda_q2, lambda_k2,
              subln_g, w_branch_a, w_branch_b, w_branch_c, w_out, ln1_g, ln1_b, router_w, router_bias,
              expert_w_gate_up, expert_w_down, shared_w_gate_up, shared_w_down, ln2_g, ln2_b):
    B, S, D = x.shape
    cos, sin = rope_tables(S, x.dtype)
    for l in range(DEPTH):
        h = hybrid_mixer(x, l, w_in[l], rel_bias[l], pool_w[l], pool_scale[l],
                         lambda_q1[l], lambda_k1[l], lambda_q2[l], lambda_k2[l], subln_g[l],
                         w_branch_a[l], w_branch_b[l], w_branch_c[l], w_out[l], cos, sin)
        x = layer_norm(DN_ALPHA * x + h, ln1_g[l], ln1_b[l])
        xf = x.reshape(B * S, D)
        idx, wts = route(xf, router_w[l], router_bias[l])
        y = (routed_experts(xf, idx, wts, expert_w_gate_up[l], expert_w_down[l])
             + shared_expert(xf, shared_w_gate_up[l], shared_w_down[l]))
        x = layer_norm(DN_ALPHA * x + y.reshape(B, S, D), ln2_g[l], ln2_b[l])
    return x


_drawn_inputs = setup_inputs


def setup_inputs(seed=0):
    import zlib

    import numpy as np

    out = dict(_drawn_inputs(seed))
    spreads = {}
    factors = {}
    for name, (base, spread) in spreads.items():
        noise = np.random.default_rng([zlib.crc32(name.encode()), seed]).standard_normal(out[name].shape)
        drawn = base * np.exp(spread * noise) if base else spread * noise
        out[name] = __import__('jax').numpy.asarray(drawn.astype(out[name].dtype))
    for name, factor in factors.items():
        out[name] = (out[name] * factor).astype(out[name].dtype)
    return out
```

```python
from contextlib import ExitStack

import concourse.bass as bass
from concourse import mybir

F32 = mybir.dt.float32
F32R = mybir.dt.float32r
BF16 = mybir.dt.bfloat16
I32 = mybir.dt.int32
ALU = mybir.AluOpType
ACT = mybir.ActivationFunctionType
AX = mybir.AxisListType.X

P = 128
D = 1024
KD = D // P
S = 256
TT = S // P
L = 2
CHUNK = 64
WIDTH = 512
KW = WIDTH // P
NE = 64
PAIRS = NE // 2
FE = 256
KF = FE // P
SLOTS = 64
ROUNDS = S // SLOTS
GROUPS = 8
TOPK_GROUPS = 4
ROUTED_SCALE = 2.5
ALPHA = (2 * L) ** 0.25
LN_EPS = 1e-5
RMS_EPS = 1e-5
REL_CLIP = 256
NEG = -1e30
POOL_WINDOWS = (2, 4, 8, 16)
ROPE_THETA = 500000.0
ROPE_DIM = 16

CONST = {}
CONST_COLS = 0
for _name, _width in (("cos", S), ("sin", S), ("ident", P), ("rotate", P), ("mask", S), ("iota", SLOTS),
                      ("earlier", GROUPS * GROUPS), ("before", P), ("ones", P), ("ramp", 4 * 16)):
    CONST[_name] = (CONST_COLS, CONST_COLS + _width)
    CONST_COLS += _width

Z_BLOCKS = [("qa", 0), ("ka", 512), ("va", 1024), ("qc", 2048), ("kc", 2560), ("vc", 3072), ("ub", 1536),
            ("ga", 3584), ("ga", 4096), ("gb", 4608), ("gb", 5120), ("gc", 5632), ("gc", 6144)]
BLOCKS = ([("z", b) for b in range(9)] + [("branch", 0)] + [("z", 9), ("z", 10), ("branch", 1)]
          + [("z", 11), ("z", 12), ("branch", 2), ("out", 0), ("out", 1), ("shared_up", 0), ("shared_down", 0)])
NB = len(BLOCKS)
WBUFS = 3
UNITS = 8


def unit(i):
    return i // 4, (i % 4) // 2, i % 2


def plan():
    sc = lambda i: [("scores", i, 0), ("scores", i, 1)]
    tr = lambda i: [("turn", i, j) for j in range(2 if unit(i)[0] == 0 else 1)]
    after = {
        6: sc(0), 7: tr(0) + sc(1), 8: [("pv", 0, 0)] + tr(1) + sc(2) + [("rope", 0, 0), ("rope", 0, 1)],
        9: [("pv", 1, 0)] + tr(2) + sc(3), 10: [("pv", 2, 0)] + tr(3) + [("rope", 1, 0), ("rope", 1, 1)],
        11: [("pv", 3, 0)], 12: sc(4), 13: tr(4) + sc(5), 14: [("pv", 4, 0)] + tr(5) + sc(6),
        15: [("pv", 5, 0)] + tr(6) + sc(7) + [("pool", 0, 0), ("pool", 1, 0)],
        16: [("pv", 6, 0)] + tr(7), 17: [("pv", 7, 0)] + [("branch", 0, j) for j in range(4)],
        18: [("rms", 0, 0), ("rms", 1, 0)],
        21: [("branch", 1, j) for j in range(4)], 25: [("branch", 2, j) for j in range(4)],
    }
    tasks = [("xt", 0, g) for g in range(4)]
    for u in range(2 * len(Z_BLOCKS)):
        tasks.append(("z", u, 0))
        tasks += after.get(u, [])
    return tasks + [("xt", 1, g) for g in range(4)] + [("router", 0, 0), ("shared", 0, 0), ("shared", 1, 0),
                                                       ("rank", 0, 0)]


PLAN = plan()
NT = len(PLAN)
ZU = 2 * len(Z_BLOCKS)
INDEX = {task: n for n, task in enumerate(PLAN)}
RING = 4
LAST_OF_BLOCK = {}
for _n, (_kind, _b) in enumerate(BLOCKS):
    if _kind == "branch":
        LAST_OF_BLOCK[_n] = ("branch", _b, 3)
    elif _kind == "shared_up":
        LAST_OF_BLOCK[_n] = ("shared", 1, 0)
BLOCK_OF_Z = {b: n for n, (kind, b) in enumerate(BLOCKS) if kind == "z"}
BLOCK_OF = {(kind, b): n for n, (kind, b) in enumerate(BLOCKS) if kind != "z"}


def build(nc, x, w_in, rel_bias, pool_w, pool_scale, lambda_q1, lambda_k1, lambda_q2, lambda_k2, subln_g,
          w_branch_a, w_branch_b, w_branch_c, w_out, ln1_g, ln1_b, router_w, router_bias,
          expert_w_gate_up, expert_w_down, shared_w_gate_up, shared_w_down, ln2_g, ln2_b, consts, lambda_init,
          out):
    with ExitStack() as ctx:
        def sb(name, shape, dt=F32):
            return ctx.enter_context(nc.sbuf_tensor(name, shape, dt))

        def sem(name):
            return ctx.enter_context(nc.semaphore(name))

        ring_w = sb("ring_w", [P, 2, 4096])
        x_tok = sb("x_tok", [P, TT, D])
        cst = sb("cst", [P, CONST_COLS])
        ln_gb = sb("ln_gb", [P, 2, D])
        pool_w_sb = sb("pool_w_sb", [P, L, KW, P])
        pool_s_sb = sb("pool_s_sb", [P, L, KW])
        subln_sb = sb("subln_sb", [P, L])
        router_sb = sb("router_sb", [P, L, KD, NE])
        rbias_sb = sb("rbias_sb", [P, L, NE])
        before_b = sb("before_b", [P, P], BF16)
        ones_b = sb("ones_b", [P, P], BF16)
        eps = sb("eps", [P, 2])
        nlam = sb("nlam", [P, L])
        lam_sum = sb("lam_sum", [P, L, 2])
        neg_max = sb("neg_max", [P, 2, 4])
        sums = sb("sums", [P, 2, 4])
        recips = sb("recips", [P, 2, 4])
        stats = sb("stats", [P, 2, 6])
        mean_var = sb("mean_var", [P, TT, 2])
        std = sb("std", [P, TT])
        rstd = sb("rstd", [P, TT])
        sel_b = sb("sel_b", [P, TT, NE], BF16)
        group_s = sb("group_s", [P, TT, GROUPS])
        group_r = sb("group_r", [P, TT, GROUPS])
        wsum = sb("wsum", [P, TT])
        count_f = sb("count_f", [P, 1])
        count_i = sb("count_i", [P, L], I32)
        slot_of = sb("slot_of", [P, TT, ROUNDS * NE + 2])
        gate_of = sb("gate_of", [P, TT, ROUNDS * NE + 2])

        def region(name, size):
            first = (nc.sbuf_base + 31) // 32 * 32
            sb(name, [P, size // 4])
            return lambda n, offset, shape, dt=F32: nc.alloc_sbuf_tensor_at(n, shape, dt, offset=first + offset)

        KB = 1024
        place = region("weights_region", 48 * KB)
        gu_a = place("gu_a", 0, [P, 2, KD, 2 * FE])
        dn_a = place("dn_a", 32 * KB, [P, 2, KF, D])
        w_hi = [place(f"w_hi{n}", 16 * n * KB, [P, KD, S], F32R) for n in range(WBUFS)]
        w_lo = [place(f"w_lo{n}", (16 * n + 8) * KB, [P, KD, S], F32R) for n in range(WBUFS)]
        place = region("x_region", 16 * KB)
        x_hi = place("x_hi", 0, [P, KD, S], F32R)
        x_lo = place("x_lo", 8 * KB, [P, KD, S], F32R)
        x_t = place("x_t", 0, [P, KD, S])
        score = place("score", 8 * KB, [P, TT, NE])
        choice = place("choice", 8 * KB + 512, [P, TT, NE])
        replaced = place("replaced", 9 * KB, [P, TT, NE])
        sel = place("sel", 9 * KB + 512, [P, TT, NE])
        top = place("top", 10 * KB, [P, TT * GROUPS, 8])
        beats = place("beats", 10 * KB + 512, [P, TT, GROUPS, GROUPS])
        ties = place("ties", 11 * KB, [P, TT, GROUPS, GROUPS])
        sh_silu = place("sh_silu", 12 * KB, [P, KF, S])[:]
        sh_t = place("sh_t", 14 * KB, [P, KF, S])[:]

        arena = sb("arena", [P, 18816])

        def view(at, *shape, dt=F32):
            size = 1
            for n in shape:
                size *= n
            words = size if dt == F32 else size // 2
            v = arena[:, at:at + words]
            if dt != F32:
                v = v.bitcast(dt)
            if len(shape) == 2:
                v = v.rearrange("p (a b) -> p a b", a=shape[0])
            elif len(shape) == 3:
                v = v.rearrange("p (a b c) -> p a b c", a=shape[0], b=shape[1])
            return v

        gu_b = view(0, 2, KD, 2 * FE)
        dn_b = view(8192, 2, KF, D)
        parts = [view(12288 + 1024 * n, TT, KD, P, dt=BF16) for n in range(3)]
        xe_t = view(15360, KD, P)
        y_sb = view(16384, D)
        gates = view(17408, TT, P)
        gates_t = view(17664, S)
        silu_g = view(17920, FE)
        hid = view(18176, FE)
        hid_t = view(18432, KF, P)
        onehot = view(18688, TT, P, dt=BF16)
        gu, dn = [gu_a[:], gu_b], [dn_a[:], dn_b]
        rest = [xe_t, y_sb.rearrange("p (a b) -> p a b", a=KD)]

        qa_t, ka_t, va = view(0, KW, S), view(1024, KW, S), view(2048, TT, WIDTH)
        qc_t, kc_t, vc = view(3072, KW, S), view(4096, KW, S), view(5120, TT, WIDTH)
        ub_t = view(6144, KW, S)
        probs = [view(7168, 4, S), view(8192, 4, S)]
        probs_t = view(9216, 4, 2, P)
        ya_t, yc_t, mixed, pooled = view(10240, KW, S), view(11264, KW, S), view(12288, KW, S), view(13312, KW, S)
        bias_rev = view(14336, 8, S)
        yb_t = view(2048, KW, S)
        sig = view(0, KD, S)
        merged = view(3072, KD, S)
        squares, rms = view(7168, KW, S), view(8192, KW, S)
        lam_in = view(12288, L, 4, CHUNK)
        q_t, k_t, v_tok, y_t = [qa_t, qc_t], [ka_t, kc_t], [va, vc], [ya_t, yc_t]
        branch_in = [ya_t, yb_t, yc_t]

        banks = [ctx.enter_context(nc.psum_tensor(f"bank{n}", [P, 512], F32)) for n in range(8)]
        acc = [[banks[2 * t + h] for h in range(2)] for t in range(TT)]
        bank_gather, bank_h, bank_y, bank_t = banks[4:8]

        def const(name):
            a, b = CONST[name]
            return cst[:, a:b]

        ident = const("ident")

        x_in = sem("x_in")
        small_in = sem("small_in")
        bias_in = sem("bias_in")
        ln_in = sem("ln_in")
        block_in = [sem("block_in0"), sem("block_in1")]
        gu_in = [sem("gu_in0"), sem("gu_in1")]
        dn_in = [sem("dn_in0"), sem("dn_in1")]
        out_done = sem("out_done")
        bank_ready = sem("bank_ready")
        bank_free = [sem(f"bank_free{n}") for n in range(RING)]
        setup_done = sem("setup_done")
        setup_pool = sem("setup_pool")
        x_hi_ready = sem("x_hi_ready")
        w_hi_ready = sem("w_hi_ready")
        w_lo_ready = sem("w_lo_ready")
        lam_ready = sem("lam_ready")
        lam_exp = sem("lam_exp")
        bias_masked = sem("bias_masked")
        max_ready = sem("max_ready")
        exp_ready = sem("exp_ready")
        recip_ready = sem("recip_ready")
        scaled = sem("scaled")
        probs_ready = sem("probs_ready")
        rope_ready = sem("rope_ready")
        mixed_ready = sem("mixed_ready")
        squares_ready = sem("squares_ready")
        yc_ready = sem("yc_ready")
        merged_ready = sem("merged_ready")
        h_ready = sem("h_ready")
        var_ready = sem("var_ready")
        std_ready = sem("std_ready")
        ln_done = sem("ln_done")
        sel_ready = sem("sel_ready")
        count_ready = sem("count_ready")
        part_ready = sem("part_ready")
        rest_ready = sem("rest_ready")
        shared_down = sem("shared_down")
        s_ready = sem("s_ready")
        sg_ready = sem("sg_ready")
        gathered = sem("gathered")
        xe_ready = sem("xe_ready")
        up_done = sem("up_done")
        silu_ready = sem("silu_ready")
        hid_ready = sem("hid_ready")
        hid_turned = sem("hid_turned")
        hid_t_ready = sem("hid_t_ready")
        gates_turned = sem("gates_turned")
        gates_t_ready = sem("gates_t_ready")
        y_done = sem("y_done")
        y_ready = sem("y_ready")
        acc_done = sem("acc_done")
        dve_step = sem("dve_step")
        loads_cleared = sem("loads_cleared")

        def at(l, task):
            n = l * NT + INDEX[task]
            return n, n % RING, n // RING

        def bank(l, task):
            return banks[4 + at(l, task)[1]]

        def wait_task(eng, l, task):
            eng.wait_ge(bank_ready, at(l, task)[0] + 1)

        def wait_evac(eng, l, task):
            _, b, uses = at(l, task)
            eng.wait_ge(bank_free[b], uses + 1)

        def free(ins, l, task):
            ins.then_inc(bank_free[at(l, task)[1]], 1)

        def rounds_of(eng, l):
            eng.wait_ge(count_ready, l + 1)
            most = eng.value_load(count_i[0:1, l:l + 1], min_val=1, max_val=S)
            return eng.snap((most + (SLOTS - 1)) >> 6).with_bounds(min_val=1, max_val=ROUNDS)

        def z_chunk(u):
            return ring_w[:, BLOCK_OF_Z[u // 2] % 2, :].rearrange("p (k n) -> p k n", k=KD)[
                :, :, S * (u % 2):S * (u % 2) + S]

        HALVES = PAIRS // 2

        def norm_std(act, l, which):
            for t in range(TT):
                act.wait_ge(var_ready, TT * (2 * l + which) + t + 1)
                nc.scalar.activation(std[:, t:t + 1], mean_var[:, t, 1:2], ACT.Sqrt,
                                     bias=eps[:, 0:1]).then_inc(std_ready, 1)

        block = ctx.enter_context(nc.Block())

        @block.sync
        def _(sp):
            sp.dma_start(x_tok[:], x.rearrange("a (t p) d -> p (a t) d", p=P)).then_inc(x_in, 16)
            sp.dma_start(cst[:], consts).then_inc(x_in, 16)

            def load_block(l, n):
                kind, b = BLOCKS[n]
                slot, before = n % 2, n - 2
                bl = l if before >= 0 else l - 1
                before %= NB
                if bl >= 0:
                    if BLOCKS[before][0] == "z":
                        sp.wait_ge(w_lo_ready, ZU * bl + 2 * BLOCKS[before][1] + 2)
                    elif before in LAST_OF_BLOCK:
                        wait_task(sp, bl, LAST_OF_BLOCK[before])
                    elif BLOCKS[before][0] == "out":
                        sp.wait_ge(h_ready, TT * bl + TT)
                    else:
                        sp.wait_ge(shared_down, bl + 1)
                if kind == "z":
                    c = Z_BLOCKS[b][1]
                    dst = ring_w[:, slot, :].rearrange("p (k n) -> p k n", k=KD)
                    src = w_in[l, :, c:c + WIDTH].rearrange("(p k) n -> p k n", k=KD)
                elif kind == "branch":
                    dst = ring_w[:, slot, :].rearrange("p (k n) -> p k n", k=KW)
                    src = (w_branch_a, w_branch_b, w_branch_c)[b][l].rearrange("(k p) n -> p k n", p=P)
                elif kind == "out":
                    dst = ring_w[:, slot, :].rearrange("p (k n) -> p k n", k=KD)
                    src = w_out[l, :, 512 * b:512 * b + 512].rearrange("(k p) n -> p k n", p=P)
                elif kind == "shared_up":
                    dst = ring_w[:, slot, :]
                    src = shared_w_gate_up[l].rearrange("(p k) n -> p (k n)", k=KD)
                else:
                    dst = ring_w[:, slot, 0:KF * D].rearrange("p (k n) -> p k n", k=KF)
                    src = shared_w_down[l].rearrange("(k p) n -> p k n", p=P)
                sp.dma_start(dst, src).then_inc(block_in[slot], 16)

            def load_pair(l, slot, pair):
                sp.dma_start(gu[slot], expert_w_gate_up[l, bass.ds(2 * pair, 2)]
                             .rearrange("e (p k) n -> p e k n", k=KD)).then_inc(gu_in[slot], 16)

            def load_down(l, slot, pair):
                sp.dma_start(dn[slot], expert_w_down[l, bass.ds(2 * pair, 2)]
                             .rearrange("e (p k) n -> p e k n", k=KF)).then_inc(dn_in[slot], 16)

            start = 0
            for l in range(L):
                load_block(l, 0)
                load_block(l, 1)
                for n in range(2, NB - 2):
                    load_block(l, n)
                wait_task(sp, l, ("z", ZU - 1, 0))
                load_pair(l, 0, 0)
                load_down(l, 0, 0)
                sp.wait_ge(h_ready, TT * l + TT)
                for n in range(NB - 2, NB):
                    load_block(l, n)
                load_pair(l, 1, 1)
                load_down(l, 1, 1)
                rounds = rounds_of(sp, l)
                with sp.Fori(0, rounds * HALVES - 1) as i:
                    done = 2 * (i + start)
                    pair = 2 * ((i + 1) & (HALVES - 1))
                    for slot in range(2):
                        sp.wait_ge(up_done, done + slot + 1)
                        sp.sem_inc(loads_cleared, 1)
                        load_pair(l, slot, pair + slot)
                        sp.wait_ge(y_done, 2 * (done + slot) + 2)
                        sp.sem_inc(loads_cleared, 1)
                        load_down(l, slot, pair + slot)
                start = start + rounds * HALVES
            for t in range(TT):
                sp.wait_ge(ln_done, TT * (2 * L - 1) + t + 1)
                sp.dma_start(out[0, P * t:P * t + P, :], x_tok[:, t, :]).then_inc(out_done, 16)
            sp.wait_ge(out_done, 16 * TT)

        @block.gpsimd
        def _(pool):
            pool.memset(slot_of[:, :, ROUNDS * NE:], -1.0).then_inc(setup_pool, 1)
            pool.memset(gate_of[:, :, ROUNDS * NE:], 0.0).then_inc(setup_pool, 1)

            def split_low(l, u):
                pool.wait_ge(w_hi_ready, ZU * l + u + 1)
                pool.tensor_tensor(w_lo[u % WBUFS][:], z_chunk(u), w_hi[u % WBUFS][:].bitcast(F32),
                                   ALU.subtract).then_inc(w_lo_ready, 1)

            for l in range(L):
                for u in range(WBUFS):
                    split_low(l, u)
                pool.wait_ge(bias_in, 16 * (l + 1))
                pool.memset(bias_rev[0:CHUNK, :, 0:CHUNK], NEG).then_inc(bias_masked, 1)
                for task in PLAN:
                    kind, i, j = task
                    if kind == "z" and i + WBUFS < ZU:
                        split_low(l, i + WBUFS)
                    if kind != "scores" or j == 0:
                        continue
                    g = l * UNITS + i
                    branch, qt, _ = unit(i)
                    W = P * (qt + 1)
                    p = probs[i % 2][:, :, 0:W]
                    pool.wait_ge(recip_ready, g + 1)
                    scale = recips[:, i % 2, :].unsqueeze(2).to_broadcast([P, 4, W])
                    ins = pool.tensor_tensor(p, p, scale, ALU.mult)
                    if branch == 0:
                        ins.then_inc(probs_ready, 1)
                    else:
                        ins.then_inc(scaled, 1)
                        pool.wait_ge(scaled, l * 4 + i - 3)
                        pool.tensor_tensor(p[:, 0::2, :], p[:, 0::2, :], p[:, 1::2, :], ALU.add).then_inc(probs_ready, 1)
                for t in range(TT):
                    for n in range(2):
                        k = 3 * TT * l + 3 * t + n
                        pool.wait_ge(part_ready, k + 1)
                        src = x_tok[:, t, :].rearrange("p (q k) -> p k q", k=KD) if n == 0 else rest[t]
                        if n:
                            pool.wait_ge(rest_ready, 2 * TT * l + 2 * t + n)
                        pool.tensor_tensor(rest[t], src, parts[n][:, t], ALU.subtract).then_inc(rest_ready, 1)
                pool.wait_ge(part_ready, 3 * TT * (l + 1))
                pool.memset(y_sb[:, 0:512], 0.0).then_inc(y_ready, 1)
                pool.memset(y_sb[:, 512:D], 0.0).then_inc(y_ready, 1)
                pool.memset(gates_t, 0.0).then_inc(gates_t_ready, 1)

        @block.scalar
        def _(act):
            def load_ln(l, which):
                g, b = ((ln1_g, ln1_b), (ln2_g, ln2_b))[which]
                act.dma_start(ln_gb[:, 0, :], g[l].partition_broadcast(P)).then_inc(ln_in, 16)
                act.dma_start(ln_gb[:, 1, :], b[l].partition_broadcast(P)).then_inc(ln_in, 16)

            def load_bias(l):
                head = 2 * REL_CLIP + 1
                rows = bass.AP(tensor=rel_bias.tensor, offset=rel_bias.offset + l * 8 * head + REL_CLIP - P + 1,
                               ap=[[1, P], [head, 8], [1, S]])
                act.dma_start(bias_rev, rows).then_inc(bias_in, 16)

            smalls = 0
            for l in range(L):
                for n, vec in enumerate((lambda_q1, lambda_k1, lambda_q2, lambda_k2)):
                    act.dma_start(lam_in[:, l, n, :], vec[l].partition_broadcast(P)).then_inc(small_in, 16)
                act.dma_start(rbias_sb[:, l, :], router_bias[l].partition_broadcast(P)).then_inc(small_in, 16)
                act.dma_start(router_sb[:, l], router_w[l].rearrange("(p k) e -> p k e", k=KD)).then_inc(small_in, 16)
                act.dma_start(pool_w_sb[:, l], pool_w[l].rearrange("g c d -> c g d")).then_inc(small_in, 16)
                with nc.allow_non_contiguous_dma(reason="a few hundred words, once"):
                    act.dma_start(pool_s_sb[:, l], pool_scale[l].rearrange("(g p) -> p g", p=P)).then_inc(small_in, 16)
                    act.dma_start(subln_sb[:, l:l + 1], subln_g[l].rearrange("(p a) -> p a", a=1)).then_inc(small_in, 16)
            load_bias(0)
            load_ln(0, 0)

            def split_high(l, u):
                n = BLOCK_OF_Z[u // 2]
                if u % 2 == 0:
                    act.wait_ge(block_in[n % 2], 16 * (l * (NB // 2) + n // 2 + 1))
                nc.scalar.copy(w_hi[u % WBUFS][:], z_chunk(u)).then_inc(w_hi_ready, 1)

            start = 0
            for l in range(L):
                for u in range(WBUFS):
                    split_high(l, u)
                for task in PLAN:
                    kind, i, j = task
                    b = bank(l, task)
                    if l == 0 and task == ("z", 4, 0):
                        act.wait_ge(lam_ready, 1)
                        nc.scalar.activation(lam_sum[:], lam_sum[:], ACT.Exp).then_inc(lam_exp, 1)
                    if kind == "xt" and i == 0:
                        wait_task(act, l, task)
                        nc.scalar.copy(x_hi[:, 2 * j:2 * j + 2, :],
                                       b[:].rearrange("p (c n) -> p c n", c=2)).then_inc(x_hi_ready, 1)
                    elif kind == "xt" and j % 2 == 0:
                        wait_task(act, l, task)
                        free(nc.scalar.copy(x_t[:, 2 * j:2 * j + 2, :], b[:].rearrange("p (c n) -> p c n", c=2)),
                             l, task)
                    elif kind == "z":
                        wait_task(act, l, task)
                        name, half = Z_BLOCKS[i // 2][0], i % 2
                        two = b[:].rearrange("p (c n) -> p c n", c=2)
                        if name in ("ga", "gb", "gc"):
                            v = (i - 14) % 4
                            if name != "ga":
                                wait_evac(act, l, ("branch", 0 if name == "gb" else 1, v))
                            ins = nc.scalar.activation(sig[:, 2 * v:2 * v + 2, :], two, ACT.Sigmoid)
                        elif name in ("va", "vc"):
                            ins = nc.scalar.copy((va if name == "va" else vc)[:, :, S * half:S * half + S], two)
                        else:
                            dst = {"qa": qa_t, "ka": ka_t, "qc": qc_t, "kc": kc_t, "ub": ub_t}[name]
                            ins = nc.scalar.copy(dst[:, 2 * half:2 * half + 2, :], two)
                        free(ins, l, task)
                        if i + WBUFS < ZU:
                            split_high(l, i + WBUFS)
                    elif kind == "scores" and j == 1:
                        g, W = l * UNITS + i, P * (unit(i)[1] + 1)
                        act.wait_ge(max_ready, g + 1)
                        for m in range(4):
                            p = probs[i % 2][:, m, 0:W]
                            ins = nc.scalar.activation(p, p, ACT.Exp, bias=neg_max[:, i % 2, m:m + 1],
                                                       accum_out=sums[:, i % 2, m:m + 1])
                        ins.then_inc(exp_ready, 1)
                    elif kind == "turn":
                        wait_task(act, l, task)
                        branch, qt, _ = unit(i)
                        s0 = 2 * j if branch == 0 else 0
                        free(nc.scalar.copy(probs_t[:, s0:s0 + 2, 0:qt + 1, :],
                                            b[:, 0:2 * (qt + 1) * P].rearrange("p (m k n) -> p m k n", m=2, k=qt + 1)),
                             l, task)
                    elif kind == "rms":
                        wait_task(act, l, task)
                        free(nc.scalar.activation(rms[:, 2 * i:2 * i + 2, :], b[:].rearrange("p (c n) -> p c n", c=2),
                                                  ACT.Sqrt, bias=eps[:, 1:2], scale=1.0 / P), l, task)
                    elif kind == "router":
                        wait_task(act, l, task)
                        free(nc.scalar.activation(score[:], b[:, 0:TT * NE].rearrange("p (t e) -> p t e", t=TT),
                                                  ACT.Exp, scale=-1.0), l, task)
                    elif kind == "shared" and i == 0:
                        wait_task(act, l, task)
                        free(nc.scalar.activation(sh_silu, b[:].rearrange("p (c n) -> p c n", c=2), ACT.Silu), l, task)
                    if task == ("branch", 2, 3):
                        norm_std(act, l, 0)
                    if task == ("xt", 1, 2):
                        act.wait_ge(ln_done, TT * 2 * l + TT)
                        load_ln(l, 1)

                for t in range(TT):
                    for n in range(3):
                        src = x_tok[:, t, :].rearrange("p (q k) -> p k q", k=KD) if n == 0 else rest[t]
                        if n:
                            act.wait_ge(rest_ready, 2 * TT * l + 2 * t + n)
                        nc.scalar.copy(parts[n][:, t], src).then_inc(part_ready, 1)

                def gather_out(n, half):
                    act.wait_ge(gathered, 2 * (n + l) + half + 1)
                    nc.scalar.copy(xe_t[:, 4 * half:4 * half + 4, :],
                                   bank_gather[:].rearrange("p (c n) -> p c n", c=4)).then_inc(xe_ready, 1)

                rounds = rounds_of(act, l)
                gather_out(2 * start, 0)
                gather_out(2 * start, 1)
                with act.Fori(0, rounds * HALVES) as i:
                    for u in range(2):
                        n = 2 * (i + start) + u
                        act.wait_ge(up_done, n + 1)
                        nc.scalar.activation(silu_g, bank_h[:, 0:FE], ACT.Silu).then_inc(silu_ready, 1)
                        gather_out(n + 1, 0)
                        gather_out(n + 1, 1)
                start = start + rounds * HALVES
                norm_std(act, l, 1)
                if l + 1 < L:
                    act.wait_ge(xe_ready, 2 * (2 * start + l) + 2)
                    act.sem_inc(loads_cleared, 1)
                    act.wait_ge(ln_done, TT * (2 * l + 1) + TT)
                    load_bias(l + 1)
                    load_ln(l + 1, 0)

        @block.vector
        def _(dve):
            steps = [0]

            def step(ins):
                ins.then_inc(dve_step, 1)
                steps[0] += 1

            def settle():
                dve.wait_ge(dve_step, steps[0])

            v = nc.vector
            dve.wait_ge(x_in, 32)
            v.tensor_copy(before_b[:], const("before")).then_inc(setup_done, 1)
            v.tensor_copy(ones_b[:], const("ones")).then_inc(setup_done, 1)
            v.memset(eps[:, 0:1], LN_EPS).then_inc(setup_done, 1)
            v.memset(eps[:, 1:2], RMS_EPS).then_inc(setup_done, 1)
            def lambdas():
                dve.wait_ge(small_in, 16 * 9 * L)
                for l in range(L):
                    step(v.tensor_tensor(lam_in[:, l, 0::2, :], lam_in[:, l, 0::2, :], lam_in[:, l, 1::2, :], ALU.mult))
                    step(v.tensor_scalar(subln_sb[:, l:l + 1], subln_sb[:, l:l + 1], 1.0 - lambda_init[l], None, ALU.mult))
                settle()
                for l in range(L):
                    ins = v.tensor_reduce(lam_sum[:, l, :], lam_in[:, l, 0::2, :], AX, ALU.add)
                    if l < L - 1:
                        step(ins)
                ins.then_inc(lam_ready, 1)
                dve.wait_ge(lam_exp, 1)
                step(v.tensor_tensor(nlam[:], lam_sum[:, :, 1], lam_sum[:, :, 0], ALU.subtract))
                settle()
                for l in range(L):
                    step(v.tensor_scalar(nlam[:, l:l + 1], nlam[:, l:l + 1], -lambda_init[l], None, ALU.add))

            def norm(l, which):
                k = 2 * l + which
                dve.wait_ge(ln_in, 32 * (k + 1))
                for t in range(TT):
                    if which == 0:
                        dve.wait_ge(h_ready, TT * l + t + 1)
                    else:
                        dve.wait_ge(acc_done, l + 1)
                    row = x_tok[:, t, :]
                    for h in range(2):
                        part = x_tok[:, t, 512 * h:512 * h + 512]
                        step(v.scalar_tensor_tensor(out=part, in0=part, scalar=ALPHA, in1=acc[t][h][:],
                                                    op0=ALU.mult, op1=ALU.add))
                    settle()
                    for h in range(2):
                        step(v.bn_stats(stats[:, h, :], x_tok[:, t, 512 * h:512 * h + 512]))
                    settle()
                    v.bn_aggr(mean_var[:, t, :], stats[:].rearrange("p a b -> p (a b)")).then_inc(var_ready, 1)
                    dve.wait_ge(std_ready, TT * k + t + 1)
                    step(v.reciprocal(rstd[:, t:t + 1], std[:, t:t + 1]))
                    settle()
                    step(v.tensor_scalar(row, row, mean_var[:, t, 0:1], rstd[:, t:t + 1], ALU.subtract, ALU.mult))
                    settle()
                    step(v.tensor_tensor(row, row, ln_gb[:, 0, :], ALU.mult))
                    settle()
                    v.tensor_tensor(row, row, ln_gb[:, 1, :], ALU.add).then_inc(ln_done, 1)

            def pool_windows(l):
                wait_evac(dve, l, ("z", 12, 0))
                wait_evac(dve, l, ("z", 13, 0))
                dve.wait_ge(rope_ready, 4 * (l + 1))
                src, dst, other = ub_t, mixed, pooled
                for level in range(4):
                    n = 1 << level
                    g = slice(level, KW)
                    step(v.tensor_tensor(dst[:, g, n:], src[:, g, n:], src[:, g, :S - n], ALU.add))
                    step(v.tensor_copy(dst[:, g, 0:n], src[:, g, 0:n]))
                    settle()
                    src, dst, other = dst, other, dst
                for g, w in enumerate(POOL_WINDOWS):
                    s = (mixed, pooled)[g % 2]
                    ramp = const("ramp")[:, 16 * g:16 * g + 16]
                    step(v.tensor_tensor(s[:, g, 0:16], s[:, g, 0:16], ramp, ALU.mult))
                settle()
                for g, w in enumerate(POOL_WINDOWS):
                    s = (mixed, pooled)[g % 2]
                    ins = v.scalar_tensor_tensor(out=mixed[:, g, :], in0=s[:, g, :], scalar=1.0 / w, in1=ub_t[:, g, :],
                                                 op0=ALU.mult, op1=ALU.subtract)
                    if g < KW - 1:
                        step(ins)
                ins.then_inc(mixed_ready, 1)

            def route(l):
                wait_evac(dve, l, ("router", 0, 0))
                step(v.tensor_scalar(score[:], score[:], 1.0, None, ALU.add))
                settle()
                step(v.reciprocal(score[:], score[:]))
                settle()
                step(v.tensor_tensor(choice[:], score[:], rbias_sb[:, l, :].unsqueeze(1).to_broadcast([P, TT, NE]),
                                     ALU.add))
                settle()
                for t in range(TT):
                    for g in range(GROUPS):
                        step(v.max(top[:, t * GROUPS + g, :], choice[:, t, 8 * g:8 * g + 8]))
                settle()
                step(v.tensor_tensor(group_s[:].rearrange("p t g -> p (t g)"), top[:, :, 0], top[:, :, 1], ALU.add))
                settle()
                one = group_s[:].unsqueeze(3).to_broadcast([P, TT, GROUPS, GROUPS])
                other = group_s[:].unsqueeze(2).to_broadcast([P, TT, GROUPS, GROUPS])
                earlier = const("earlier").unsqueeze(1).to_broadcast([P, TT, GROUPS * GROUPS])
                step(v.tensor_tensor(beats[:], other, one, ALU.is_gt))
                step(v.tensor_tensor(ties[:], other, one, ALU.is_equal))
                settle()
                flat = ties[:].rearrange("p t a b -> p t (a b)")
                step(v.tensor_tensor(flat, flat, earlier, ALU.mult))
                settle()
                step(v.tensor_tensor(beats[:], beats[:], ties[:], ALU.add))
                settle()
                step(v.tensor_reduce(group_r[:], beats[:], AX, ALU.add))
                settle()
                step(v.tensor_scalar(group_r[:], group_r[:], TOPK_GROUPS - 0.5, NEG, ALU.is_gt, ALU.mult))
                settle()
                by_group = choice[:].rearrange("p t (g e) -> p (t g) e", g=GROUPS)
                out_of = group_r[:].rearrange("p t g -> p (t g)").unsqueeze(2).to_broadcast([P, TT * GROUPS, 8])
                step(v.tensor_tensor(by_group, by_group, out_of, ALU.add))
                settle()
                for t in range(TT):
                    step(v.max(top[:, t, :], choice[:, t, :]))
                settle()
                for t in range(TT):
                    step(v.match_replace(out=replaced[:, t, :], in_to_replace=top[:, t, :], in_values=choice[:, t, :],
                                         imm_value=3 * NEG))
                settle()
                v.tensor_tensor(sel_b[:], replaced[:], choice[:], ALU.not_equal).then_inc(sel_ready, 1)
                step(v.tensor_tensor(sel[:], replaced[:], choice[:], ALU.not_equal))
                settle()
                step(v.tensor_tensor(score[:], score[:], sel[:], ALU.mult))
                settle()
                step(v.tensor_reduce(wsum[:], score[:], AX, ALU.add))
                settle()
                step(v.reciprocal(wsum[:], wsum[:]))
                settle()
                for t in range(TT):
                    step(v.tensor_scalar(gate_of[:, t, 0:NE], score[:, t, :], wsum[:, t:t + 1], ROUTED_SCALE,
                                         ALU.mult, ALU.mult))
                settle()
                for r in range(1, ROUNDS):
                    step(v.tensor_copy(gate_of[:, :, r * NE:(r + 1) * NE], gate_of[:, :, 0:NE]))
                step(v.tensor_scalar(choice[:], sel[:], 1000.0, -1000.0, ALU.mult, ALU.add))
                settle()

            def ranks(l):
                task = ("rank", 0, 0)
                b = bank(l, task)
                wait_task(dve, l, task)
                step(v.tensor_tensor(slot_of[:, :, 0:NE], b[:, 0:TT * NE].rearrange("p (t e) -> p t e", t=TT), sel[:],
                                     ALU.mult))
                free(v.tensor_reduce(count_f[:], b[:, TT * NE:(TT + 1) * NE], AX, ALU.max), l, task)
                settle()
                step(v.tensor_tensor(slot_of[:, :, 0:NE], slot_of[:, :, 0:NE], choice[:], ALU.add))
                wait_evac(dve, l, task)
                v.tensor_copy(count_i[:, l:l + 1], count_f[:]).then_inc(count_ready, 1)
                settle()
                for r in range(1, ROUNDS):
                    step(v.tensor_scalar(slot_of[:, :, r * NE:(r + 1) * NE], slot_of[:, :, 0:NE], float(-SLOTS * r), None,
                                         ALU.add))
                settle()

            def slots(n, l, col):
                iota = const("iota").unsqueeze(1).unsqueeze(1).to_broadcast([P, TT, 2, SLOTS])
                rank = slot_of[:, :, bass.ds(col, 2)].unsqueeze(3).to_broadcast([P, TT, 2, SLOTS])
                gate = gate_of[:, :, bass.ds(col, 2)].unsqueeze(3).to_broadcast([P, TT, 2, SLOTS])
                hot = onehot.rearrange("p t (e c) -> p t e c", e=2)
                if not isinstance(n, int) or n + l:
                    dve.wait_ge(sg_ready, n + l)
                v.tensor_tensor(hot, rank, iota, ALU.is_equal).then_inc(s_ready, 1)
                dve.wait_ge(s_ready, n + l + 1)
                v.tensor_tensor(gates.rearrange("p t (e c) -> p t e c", e=2), hot, gate, ALU.mult).then_inc(sg_ready, 1)

            start = 0
            for l in range(L):
                for task in PLAN:
                    kind, i, j = task
                    b = bank(l, task)
                    pair = b[:].rearrange("p (c n) -> p c n", c=2)
                    if kind == "xt" and i == 0:
                        dve.wait_ge(x_hi_ready, 4 * l + j + 1)
                        free(v.tensor_tensor(x_lo[:, 2 * j:2 * j + 2, :], pair,
                                             x_hi[:, 2 * j:2 * j + 2, :].bitcast(F32), ALU.subtract), l, task)
                        if (l, j) == (0, 3):
                            lambdas()
                    elif kind == "xt" and j % 2 == 1:
                        wait_task(dve, l, task)
                        free(v.tensor_copy(x_t[:, 2 * j:2 * j + 2, :], pair), l, task)
                    elif kind == "scores":
                        branch, qt, g = unit(i)
                        W = P * (qt + 1)
                        wait_task(dve, l, task)
                        if i >= 2:
                            wait_task(dve, l, ("turn", i - 2, 1 if unit(i - 2)[0] == 0 else 0))
                        if branch == 0:
                            if (i, j) == (0, 0):
                                dve.wait_ge(bias_masked, l + 1)
                            m = 4 * g + j
                            add = bias_rev[:, m:m + 3:2, 0:W][:, :, ::-1]
                        else:
                            add = const("mask")[:, S - W:S].unsqueeze(1).to_broadcast([P, 2, W])
                        free(v.scalar_tensor_tensor(out=probs[i % 2][:, j::2, 0:W],
                                                    in0=b[:, 0:2 * W].rearrange("p (m n) -> p m n", m=2),
                                                    scalar=float(CHUNK) ** -0.5, in1=add, op0=ALU.mult, op1=ALU.add),
                             l, task)
                        if j == 1:
                            wait_evac(dve, l, ("scores", i, 0))
                            wait_evac(dve, l, task)
                            v.tensor_reduce(neg_max[:, i % 2, :], probs[i % 2][:, :, 0:W], AX, ALU.max,
                                            negate=True).then_inc(max_ready, 1)
                            dve.wait_ge(exp_ready, l * UNITS + i + 1)
                            ins = v.reciprocal(recips[:, i % 2, :], sums[:, i % 2, :])
                            if branch == 1:
                                step(ins)
                                settle()
                                odd = recips[:, i % 2, 1::2]
                                ins = v.tensor_scalar(odd, odd, nlam[:, l:l + 1], None, ALU.mult)
                            ins.then_inc(recip_ready, 1)
                    elif kind == "pv":
                        branch, qt, g = unit(i)
                        wait_task(dve, l, task)
                        free(v.tensor_copy(y_t[branch][:, 2 * g:2 * g + 2, P * qt:P * qt + P],
                                           b[:, 0:2 * P].rearrange("p (c n) -> p c n", c=2)), l, task)
                        if i == 7:
                            for k in range(4, 8):
                                wait_evac(dve, l, ("pv", k, 0))
                            v.tensor_tensor(squares, yc_t, yc_t, ALU.mult).then_inc(squares_ready, 1)
                    elif kind == "rope":
                        raw = (qc_t, kc_t)[i][:, 2 * j:2 * j + 2, :]
                        wait_task(dve, l, task)
                        if 4 * l + 2 * i + j:
                            dve.wait_ge(rope_ready, 4 * l + 2 * i + j)
                        turned = pooled[:, 0:2, :]
                        plain = pooled[:, 2:4, :]
                        free(v.tensor_tensor(turned, pair, const("sin").unsqueeze(1).to_broadcast([P, 2, S]), ALU.mult),
                             l, task)
                        step(v.tensor_tensor(plain, raw, const("cos").unsqueeze(1).to_broadcast([P, 2, S]), ALU.mult))
                        settle()
                        wait_evac(dve, l, task)
                        v.tensor_tensor(raw, plain, turned, ALU.add).then_inc(rope_ready, 1)
                    elif kind == "pool":
                        wait_task(dve, l, task)
                        for c in range(2):
                            g = 2 * i + c
                            ins = v.tensor_scalar(yb_t[:, g, :], b[:, S * c:S * c + S], pool_s_sb[:, l, g:g + 1], None,
                                                  ALU.mult)
                        free(ins, l, task)
                    elif kind == "rms":
                        wait_evac(dve, l, task)
                        r, y = rms[:, 2 * i:2 * i + 2, :], yc_t[:, 2 * i:2 * i + 2, :]
                        step(v.reciprocal(r, r))
                        settle()
                        v.scalar_tensor_tensor(out=y, in0=y, scalar=subln_sb[:, l:l + 1], in1=r, op0=ALU.mult,
                                               op1=ALU.mult).then_inc(yc_ready, 1)
                    elif kind == "branch":
                        wait_task(dve, l, task)
                        wait_evac(dve, l, ("z", 14 + 4 * i + j, 0))
                        if i:
                            settle()
                        s, m = sig[:, 2 * j:2 * j + 2, :], merged[:, 2 * j:2 * j + 2, :]
                        if i == 0:
                            free(v.tensor_tensor(m, pair, s, ALU.mult), l, task)
                        else:
                            add = pooled[:, 2 * (j % 2):2 * (j % 2) + 2, :]
                            if i == 2 and j >= 2:
                                dve.wait_ge(merged_ready, 4 * l + j - 1)
                            free(v.tensor_tensor(add, pair, s, ALU.mult), l, task)
                            wait_evac(dve, l, task)
                            if i == 1:
                                wait_evac(dve, l, ("branch", 0, j))
                            ins = v.tensor_tensor(m, m, add, ALU.add)
                            if i == 1:
                                step(ins)
                            else:
                                ins.then_inc(merged_ready, 1)
                    elif kind == "shared" and i == 1:
                        wait_task(dve, l, task)
                        wait_evac(dve, l, ("shared", 0, 0))
                        free(v.tensor_tensor(sh_t, sh_silu, pair, ALU.mult), l, task)
                    if task == ("z", 13, 0):
                        pool_windows(l)
                    if task == ("branch", 2, 3):
                        norm(l, 0)
                    if task == ("router", 0, 0):
                        route(l)
                    if task == ("rank", 0, 0):
                        ranks(l)

                dve.wait_ge(setup_pool, 2)
                slots(2 * start, l, 0)
                rounds = rounds_of(dve, l)
                with dve.Fori(0, rounds * HALVES) as i:
                    for u in range(2):
                        n = 2 * (i + start) + u
                        dve.wait_ge(silu_ready, n + 1)
                        v.tensor_tensor(hid, silu_g, bank_h[:, FE:2 * FE], ALU.mult).then_inc(hid_ready, 1)
                        dve.wait_ge(hid_turned, n + 1)
                        v.tensor_copy(hid_t, bank_t[:, 0:FE].rearrange("p (k n) -> p k n", k=KF)).then_inc(hid_t_ready, 1)
                        dve.wait_ge(gates_turned, n + 1)
                        v.tensor_copy(gates_t, bank_t[:, FE:FE + S]).then_inc(gates_t_ready, 1)
                        slots(n + 1, l, 4 * i + 2 * u + 2)
                        for h in range(2):
                            dve.wait_ge(y_done, 2 * n + h + 1)
                            v.tensor_copy(y_sb[:, 512 * h:512 * h + 512], bank_y[:]).then_inc(y_ready, 1)
                start = start + rounds * HALVES
                norm(l, 1)

        @block.tensor
        def _(pe):
            mm = nc.tensor.matmul
            pe.wait_ge(setup_done, 4)

            def acquire(l, task):
                n, b, uses = at(l, task)
                if uses:
                    pe.wait_ge(bank_free[b], uses)

            def block_ready(l, n):
                pe.wait_ge(block_in[n % 2], 16 * (l * (NB // 2) + n // 2 + 1))

            def slot_of_block(n, k):
                return ring_w[:, n % 2, :].rearrange("p (k n) -> p k n", k=k)

            start = 0
            for l in range(L):
                for task in PLAN:
                    kind, i, j = task
                    if task == ("xt", 1, 0):
                        pe.wait_ge(merged_ready, 4 * (l + 1))
                        for t in range(TT):
                            for h in range(2):
                                n = BLOCK_OF["out", h]
                                if t == 0:
                                    block_ready(l, n)
                                for k in range(KD):
                                    ins = mm(acc[t][h][:], merged[:, k, P * t:P * t + P], slot_of_block(n, KD)[:, k, :],
                                             start=(k == 0), stop=(k == KD - 1))
                            ins.then_inc(h_ready, 1)
                    if kind == "rank":
                        n = BLOCK_OF["shared_down", 0]
                        block_ready(l, n)
                        wait_evac(pe, l, ("shared", 1, 0))
                        for t in range(TT):
                            for h in range(2):
                                for k in range(KF):
                                    ins = mm(acc[t][h][:], sh_t[:, k, P * t:P * t + P],
                                             ring_w[:, n % 2, D * k + 512 * h:D * k + 512 * h + 512],
                                             start=(k == 0), stop=(k == KF - 1))
                        ins.then_inc(shared_down, 1)
                    acquire(l, task)
                    b = bank(l, task)
                    if kind == "xt":
                        if i == 0 and j == 0:
                            if l == 0:
                                pe.wait_ge(x_in, 32)
                            else:
                                pe.wait_ge(ln_done, TT * 2 * l)
                        if i == 1 and j == 0:
                            pe.wait_ge(ln_done, TT * (2 * l + 1))
                        for c in range(2):
                            for t in range(TT):
                                ins = nc.tensor.transpose(b[:, S * c + P * t:S * c + P * t + P],
                                                          x_tok[:, t, 2 * j + c::KD], ident)
                    elif kind == "z":
                        if i == 0:
                            for g in range(4):
                                wait_evac(pe, l, ("xt", 0, g))
                        pe.wait_ge(w_lo_ready, ZU * l + i + 1)
                        hi, lo = w_hi[i % WBUFS], w_lo[i % WBUFS]
                        by_token = Z_BLOCKS[i // 2][0] in ("va", "vc")
                        for c in range(2):
                            cols = slice(P * c, P * c + P)
                            for k in range(KD):
                                for a, w in ((0, 0), (0, 1), (1, 0)):
                                    wk, xk = (hi, lo)[a][:, k, :], (x_hi, x_lo)[w][:, k, :]
                                    if by_token:
                                        lhs, rhs = (x_hi, x_lo)[a][:, k, cols], (hi, lo)[w][:, k, :]
                                    else:
                                        lhs, rhs = wk[:, cols], xk
                                    ins = mm(b[:, S * c:S * c + S], lhs, rhs, start=(k == 0 and a + w == 0),
                                             stop=(k == KD - 1 and a == 1))
                    elif kind == "scores":
                        branch, qt, g = unit(i)
                        W = P * (qt + 1)
                        if branch == 0 and i == 0 and j == 0:
                            for u in range(4):
                                wait_evac(pe, l, ("z", u, 0))
                        if branch == 1:
                            pe.wait_ge(rope_ready, 4 * (l + 1))
                        rows = slice(CHUNK * j, CHUNK * j + CHUNK)
                        for m in range(2):
                            ins = mm(b[:, W * m:W * m + W], q_t[branch][rows, 2 * g + m, P * qt:P * qt + P],
                                     k_t[branch][rows, 2 * g + m, 0:W], start=True, stop=True)
                    elif kind == "turn":
                        branch, qt, g = unit(i)
                        pe.wait_ge(probs_ready, l * UNITS + i + 1)
                        maps = (2 * j, 2 * j + 1) if branch == 0 else (0, 2)
                        for n, m in enumerate(maps):
                            for kt in range(qt + 1):
                                c = P * (n * (qt + 1) + kt)
                                ins = nc.tensor.transpose(b[:, c:c + P], probs[i % 2][:, m, P * kt:P * kt + P], ident)
                    elif kind == "pv":
                        branch, qt, g = unit(i)
                        for k in range(2 if branch == 0 else 1):
                            wait_evac(pe, l, ("turn", i, k))
                        if i in (0, 4):
                            first = 4 if branch == 0 else 10
                            wait_evac(pe, l, ("z", first, 0))
                            wait_evac(pe, l, ("z", first + 1, 0))
                        for m in range(4 if branch == 0 else 2):
                            for kt in range(qt + 1):
                                if branch == 0:
                                    o = b[CHUNK * (m % 2):CHUNK * (m % 2) + CHUNK, P * (m // 2):P * (m // 2) + P]
                                    val = va[:, kt, CHUNK * (4 * g + m):CHUNK * (4 * g + m) + CHUNK]
                                else:
                                    o = b[:, P * m:P * m + P]
                                    val = vc[:, kt, P * (2 * g + m):P * (2 * g + m) + P]
                                ins = mm(o, val, probs_t[:, m, kt, :], start=(kt == 0), stop=(kt == qt))
                    elif kind == "rope":
                        wait_evac(pe, l, ("z", (6, 8)[i] + j, 0))
                        for c in range(2):
                            ins = mm(b[:, S * c:S * c + S], const("rotate"), (qc_t, kc_t)[i][:, 2 * j + c, :],
                                     start=True, stop=True)
                    elif kind == "pool":
                        pe.wait_ge(mixed_ready, l + 1)
                        if l == 0:
                            pe.wait_ge(small_in, 16 * 9 * L)
                        for c in range(2):
                            g = 2 * i + c
                            ins = mm(b[:, S * c:S * c + S], pool_w_sb[:, l, g, :], mixed[:, g, :], start=True, stop=True)
                    elif kind == "rms":
                        pe.wait_ge(squares_ready, l + 1)
                        for c in range(2):
                            ins = mm(b[:, S * c:S * c + S], const("ones"), squares[:, 2 * i + c, :], start=True, stop=True)
                    elif kind == "branch":
                        n = BLOCK_OF["branch", i]
                        if j == 0:
                            block_ready(l, n)
                            if i == 0:
                                for k in range(4):
                                    wait_evac(pe, l, ("pv", k, 0))
                            elif i == 1:
                                wait_evac(pe, l, ("pool", 0, 0))
                                wait_evac(pe, l, ("pool", 1, 0))
                            else:
                                pe.wait_ge(yc_ready, 2 * (l + 1))
                        w = slot_of_block(n, KW)
                        for c in range(2):
                            col = P * (2 * j + c)
                            for k in range(KW):
                                ins = mm(b[:, S * c:S * c + S], w[:, k, col:col + P], branch_in[i][:, k, :],
                                         start=(k == 0), stop=(k == KW - 1))
                    elif kind == "router":
                        for g in range(4):
                            wait_evac(pe, l, ("xt", 1, g))
                        for t in range(TT):
                            for k in range(KD):
                                ins = mm(b[:, NE * t:NE * t + NE], x_t[:, k, P * t:P * t + P], router_sb[:, l, k, :],
                                         start=(k == 0), stop=(k == KD - 1))
                    elif kind == "shared":
                        n = BLOCK_OF["shared_up", 0]
                        if i == 0:
                            block_ready(l, n)
                        for c in range(2):
                            col = FE * i + P * c
                            for k in range(KD):
                                ins = mm(b[:, S * c:S * c + S], slot_of_block(n, KD)[:, k, col:col + P], x_t[:, k, :],
                                         start=(k == 0), stop=(k == KD - 1))
                    elif kind == "rank":
                        pe.wait_ge(sel_ready, l + 1)
                        mm(b[:, 0:NE], before_b[:], sel_b[:, 0, :], start=True, stop=True)
                        mm(b[:, NE:2 * NE], ones_b[:], sel_b[:, 0, :], start=True, stop=False)
                        mm(b[:, NE:2 * NE], before_b[:], sel_b[:, 1, :], start=False, stop=True)
                        mm(b[:, 2 * NE:3 * NE], ones_b[:], sel_b[:, 0, :], start=True, stop=False)
                        ins = mm(b[:, 2 * NE:3 * NE], ones_b[:], sel_b[:, 1, :], start=False, stop=True)
                    ins.then_inc(bank_ready, 1)

                def gather(n, half):
                    for c in range(4):
                        k = 4 * half + c
                        for t in range(TT):
                            for part in range(3):
                                ins = mm(bank_gather[:, P * c:P * c + P], parts[part][:, t, k, :], onehot[:, t, :],
                                         start=(t == 0 and part == 0), stop=(t == TT - 1 and part == 2))
                    ins.then_inc(gathered, 1)

                def combine(half):
                    for t in range(TT):
                        ins = mm(acc[t][half][:], gates_t[:, P * t:P * t + P], y_sb[:, 512 * half:512 * half + 512],
                                 start=False, stop=True, skip_group_check=True)
                    return ins

                rounds = rounds_of(pe, l)
                for task in PLAN[-RING:]:
                    wait_evac(pe, l, task)
                pe.wait_ge(part_ready, 3 * TT * (l + 1))
                pe.wait_ge(s_ready, 2 * start + l + 1)
                gather(2 * start, 0)
                pe.wait_ge(xe_ready, 2 * (2 * start + l) + 1)
                gather(2 * start, 1)
                with pe.Fori(0, rounds * HALVES) as i:
                    for u in range(2):
                        n = 2 * (i + start) + u
                        pe.wait_ge(gu_in[u], 16 * (i + start) + 16)
                        for k in range(KD):
                            if k % 4 == 0:
                                pe.wait_ge(xe_ready, 2 * (n + l) + k // 4 + 1)
                            for e in range(2):
                                ins = mm(bank_h[SLOTS * e:SLOTS * e + SLOTS, :], xe_t[:, k, SLOTS * e:SLOTS * e + SLOTS],
                                         gu[u][:, e, k, :], start=(k == 0), stop=(k == KD - 1))
                        ins.then_inc(up_done, 1)
                        pe.wait_ge(y_ready, 2 * (n + l) + 1)
                        pe.wait_ge(gates_t_ready, n + l + 1)
                        combine(0)
                        pe.wait_ge(hid_ready, n + 1)
                        for k in range(KF):
                            ins = nc.tensor.transpose(bank_t[:, P * k:P * k + P], hid[:, k::KF], ident)
                        ins.then_inc(hid_turned, 1)
                        pe.wait_ge(y_ready, 2 * (n + l) + 2)
                        combine(1)
                        pe.wait_ge(hid_t_ready, n + 1)
                        pe.wait_ge(sg_ready, n + l + 1)
                        for t in range(TT):
                            ins = nc.tensor.transpose(bank_t[:, FE + P * t:FE + P * t + P], gates[:, t, :], ident)
                        ins.then_inc(gates_turned, 1)
                        pe.wait_ge(dn_in[u], 16 * (i + start) + 16)
                        for h in range(2):
                            if h:
                                pe.wait_ge(y_ready, 2 * (n + l) + 3)
                            for k in range(KF):
                                for e in range(2):
                                    ins = mm(bank_y[SLOTS * e:SLOTS * e + SLOTS, :],
                                             hid_t[:, k, SLOTS * e:SLOTS * e + SLOTS],
                                             dn[u][:, e, k, 512 * h:512 * h + 512], start=(k == 0), stop=(k == KF - 1))
                            ins.then_inc(y_done, 1)
                            if h == 0:
                                pe.wait_ge(s_ready, n + l + 2)
                            else:
                                pe.wait_ge(xe_ready, 2 * (n + 1 + l) + 1)
                            gather(n + 1, h)
                start = start + rounds * HALVES
                pe.wait_ge(gates_t_ready, 2 * start + l + 1)
                pe.wait_ge(y_ready, 2 * (2 * start + l) + 1)
                combine(0)
                pe.wait_ge(y_ready, 2 * (2 * start + l) + 2)
                combine(1).then_inc(acc_done, 1)
                pe.wait_ge(xe_ready, 2 * (2 * start + l) + 2)


def _constants():
    import numpy as np

    c = np.zeros((P, CONST_COLS), np.float32)

    def put(name, value):
        a, b = CONST[name]
        c[:, a:b] = value

    p = np.arange(P)
    half = ROPE_DIM // 2
    inv = np.float32(ROPE_THETA) ** (-np.arange(0, ROPE_DIM, 2, dtype=np.float32) / np.float32(ROPE_DIM))
    ang = np.arange(S, dtype=np.float32)[:, None] * inv[None, :].astype(np.float32)
    cos, sin = np.ones((P, S), np.float32), np.zeros((P, S), np.float32)
    rotate = np.zeros((P, P), np.float32)
    for base in (0, CHUNK):
        for n in range(half):
            for at in (base + n, base + half + n):
                cos[at], sin[at] = np.cos(ang[:, n]), np.sin(ang[:, n])
            rotate[base + half + n, base + n] = -1.0
            rotate[base + n, base + half + n] = 1.0
    put("cos", cos)
    put("sin", sin)
    put("rotate", rotate)
    put("ident", np.eye(P, dtype=np.float32))
    mask = np.zeros((P, S), np.float32)
    mask[:CHUNK, S - CHUNK:] = NEG
    put("mask", mask)
    put("iota", np.arange(SLOTS, dtype=np.float32)[None, :])
    g = np.arange(GROUPS)
    put("earlier", (g[None, :] < g[:, None]).astype(np.float32).reshape(1, -1))
    put("before", (p[:, None] < p[None, :]).astype(np.float32))
    put("ones", 1.0)
    t = np.arange(16)
    put("ramp", np.concatenate([w / np.minimum(t + 1, w) for w in POOL_WINDOWS]).astype(np.float32)[None, :])
    return c


_INS = ["x", "w_in", "rel_bias", "pool_w", "pool_scale", "lambda_q1", "lambda_k1", "lambda_q2", "lambda_k2",
        "subln_g", "w_branch_a", "w_branch_b", "w_branch_c", "w_out", "ln1_g", "ln1_b", "router_w", "router_bias",
        "expert_w_gate_up", "expert_w_down", "shared_w_gate_up", "shared_w_down", "ln2_g", "ln2_b"]


def kernel(**inputs):
    import numpy as _np
    import concourse.bacc as _bacc
    from concourse import mybir as _mybir
    from concourse.bass_utils import run_bass_kernel_spmd as _run

    nc = _bacc.Bacc("TRN2", target_bir_lowering=False, num_devices=1)
    arrays, args = {}, []
    for name in _INS:
        a = _np.ascontiguousarray(inputs[name])
        arrays[f"in_{name}"] = a
        args.append(nc.dram_tensor(f"in_{name}", a.shape, _mybir.dt.from_np(a.dtype), kind="ExternalInput").ap())
    table = _constants()
    arrays["in_consts"] = table
    args.append(nc.dram_tensor("in_consts", table.shape, _mybir.dt.from_np(table.dtype), kind="ExternalInput").ap())
    args.append([0.8 - 0.6 * float(_np.exp(-0.3 * l)) for l in range(L)])
    args.append(nc.dram_tensor("out_0", (1, S, D), _mybir.dt.float32, kind="ExternalOutput").ap())
    build(nc, *args)
    r = _run(nc, [arrays], core_ids=[0])
    return r.results[0]["out_0"]
```

```python
from contextlib import ExitStack

import concourse.bass as bass
from concourse import mybir

F32 = mybir.dt.float32
F32R = mybir.dt.float32r
BF16 = mybir.dt.bfloat16
I32 = mybir.dt.int32
ALU = mybir.AluOpType
ACT = mybir.ActivationFunctionType
AX = mybir.AxisListType.X

P = 128
D = 1024
KD = D // P
S = 256
TT = S // P
L = 2
CHUNK = 64
WIDTH = 512
KW = WIDTH // P
NE = 64
PAIRS = NE // 2
FE = 256
KF = FE // P
SLOTS = 64
ROUNDS = S // SLOTS
GROUPS = 8
TOPK_GROUPS = 4
ROUTED_SCALE = 2.5
ALPHA = (2 * L) ** 0.25
LN_EPS = 1e-5
RMS_EPS = 1e-5
REL_CLIP = 256
NEG = -1e30
POOL_WINDOWS = (2, 4, 8, 16)
ROPE_THETA = 500000.0
ROPE_DIM = 16

CONST = {}
CONST_COLS = 0
for _name, _width in (("ident", P), ("cos", S), ("sin", S), ("rotate", P), ("mask", S), ("iota", SLOTS),
                      ("earlier", GROUPS * GROUPS), ("before", P), ("ones", P), ("ramp", 4 * 16)):
    CONST[_name] = (CONST_COLS, CONST_COLS + _width)
    CONST_COLS += _width

Z_BLOCKS = [("qa", 0), ("ka", 512), ("va", 1024), ("qc", 2048), ("kc", 2560), ("vc", 3072), ("ub", 1536),
            ("ga", 3584), ("ga", 4096), ("gb", 4608), ("gb", 5120), ("gc", 5632), ("gc", 6144)]
BLOCKS = ([("z", b) for b in range(10)] + [("branch", 0), ("z", 10), ("z", 11), ("branch", 1), ("z", 12),
          ("branch", 2), ("out", 0), ("out", 1), ("shared_up", 0), ("shared_down", 0)])
NB = len(BLOCKS)
WBUFS = 3
UNITS = 8


def unit(i):
    return i // 4, (i % 4) // 2, i % 2


def plan():
    sc = lambda i: [("scores", i, 0), ("scores", i, 1)]
    tr = lambda i: [("turn", i, j) for j in range(2 if unit(i)[0] == 0 else 1)]
    after = {
        4: sc(0), 5: sc(1), 6: tr(0) + sc(2), 7: [("pv", 0, 0)] + tr(1) + sc(3),
        8: [("pv", 1, 0)] + tr(2) + [("rope", 0, 0), ("rope", 0, 1)], 9: [("pv", 2, 0)] + tr(3),
        10: [("pv", 3, 0), ("rope", 1, 0), ("rope", 1, 1)], 11: sc(4), 12: sc(5), 13: tr(4) + sc(6),
        14: [("pv", 4, 0)] + tr(5) + sc(7), 15: [("pv", 5, 0)] + tr(6), 16: [("pv", 6, 0)] + tr(7),
        17: [("pv", 7, 0)] + [("branch", 0, j) for j in range(4)], 18: [("pool", 0, 0), ("pool", 1, 0)],
        19: [("rms", 0, 0), ("rms", 1, 0)],
        21: [("branch", 1, j) for j in range(4)], 25: [("branch", 2, j) for j in range(4)],
    }
    tasks = [("xt", 0, g) for g in range(4)]
    for u in range(2 * len(Z_BLOCKS)):
        tasks.append(("z", u, 0))
        tasks += after.get(u, [])
    return tasks + [("xt", 1, g) for g in range(4)] + [("router", 0, 0), ("shared", 0, 0), ("shared", 1, 0),
                                                       ("rank", 0, 0)]


PLAN = plan()
NT = len(PLAN)
ZU = 2 * len(Z_BLOCKS)
INDEX = {task: n for n, task in enumerate(PLAN)}
RING = 4
LAST_OF_BLOCK = {}
for _n, (_kind, _b) in enumerate(BLOCKS):
    if _kind == "branch":
        LAST_OF_BLOCK[_n] = ("branch", _b, 3)
    elif _kind == "shared_up":
        LAST_OF_BLOCK[_n] = ("shared", 1, 0)
BLOCK_OF_Z = {b: n for n, (kind, b) in enumerate(BLOCKS) if kind == "z"}
BLOCK_OF = {(kind, b): n for n, (kind, b) in enumerate(BLOCKS) if kind != "z"}


def build(nc, x, w_in, rel_bias, pool_w, pool_scale, lambda_q1, lambda_k1, lambda_q2, lambda_k2, subln_g,
          w_branch_a, w_branch_b, w_branch_c, w_out, ln1_g, ln1_b, router_w, router_bias,
          expert_w_gate_up, expert_w_down, shared_w_gate_up, shared_w_down, ln2_g, ln2_b, consts, lambda_init,
          out):
    with ExitStack() as ctx:
        def sb(name, shape, dt=F32):
            return ctx.enter_context(nc.sbuf_tensor(name, shape, dt))

        def sem(name):
            return ctx.enter_context(nc.semaphore(name))

        ring_w = sb("ring_w", [P, 2, 4096])
        x_tok = sb("x_tok", [P, TT, D])
        cst = sb("cst", [P, CONST_COLS])
        ln_gb = sb("ln_gb", [P, 2, D])
        pool_w_sb = sb("pool_w_sb", [P, KW, P])
        pool_s_sb = sb("pool_s_sb", [P, L, KW])
        subln_sb = sb("subln_sb", [P, L])
        router_sb = sb("router_sb", [P, KD, NE])
        rbias_sb = sb("rbias_sb", [P, L, NE])
        before_b = sb("before_b", [P, P], BF16)
        ones_b = sb("ones_b", [P, P], BF16)
        ident_b = sb("ident_b", [P, P], BF16)
        gate_s = sb("gate_s", [P, 1])
        eps = sb("eps", [P, 2])
        nlam = sb("nlam", [P, L])
        lam_sum = sb("lam_sum", [P, L, 2])
        neg_max = sb("neg_max", [P, 2, 4])
        sums = sb("sums", [P, 2, 4])
        recips = sb("recips", [P, 2, 4])
        stats = sb("stats", [P, 2, 6])
        mean_var = sb("mean_var", [P, TT, 2])
        std = sb("std", [P, TT])
        rstd = sb("rstd", [P, TT])
        sel_b = sb("sel_b", [P, TT, NE], BF16)
        group_s = sb("group_s", [P, TT, GROUPS])
        group_r = sb("group_r", [P, TT, GROUPS])
        wsum = sb("wsum", [P, TT])
        count_f = sb("count_f", [P, 1])
        count_i = sb("count_i", [P, L], I32)
        slot_of = sb("slot_of", [P, TT, ROUNDS * NE + 2])
        gate_of = sb("gate_of", [P, TT, ROUNDS * NE + 2])

        def region(name, size):
            first = (nc.sbuf_base + 31) // 32 * 32
            sb(name, [P, size // 4])
            return lambda n, offset, shape, dt=F32: nc.alloc_sbuf_tensor_at(n, shape, dt, offset=first + offset)

        KB = 1024
        place = region("weights_region", 48 * KB)
        gu_a = place("gu_a", 0, [P, 2, KD, 2 * FE])
        dn_a = place("dn_a", 32 * KB, [P, 2, KF, D])
        w_hi = [place(f"w_hi{n}", 16 * n * KB, [P, KD, S], F32R) for n in range(WBUFS)]
        w_lo = [place(f"w_lo{n}", (16 * n + 8) * KB, [P, KD, S], F32R) for n in range(WBUFS)]
        place = region("x_region", 16 * KB)
        x_hi = place("x_hi", 0, [P, KD, S], F32R)
        x_lo = place("x_lo", 8 * KB, [P, KD, S], F32R)
        x_t = place("x_t", 0, [P, KD, S])
        dn_c = place("dn_c", 0, [P, 2, KF, D])
        score = place("score", 8 * KB, [P, TT, NE])
        choice = place("choice", 8 * KB + 512, [P, TT, NE])
        replaced = place("replaced", 9 * KB, [P, TT, NE])
        sel = place("sel", 9 * KB + 512, [P, TT, NE])
        top = place("top", 10 * KB, [P, TT * GROUPS, 8])
        beats = place("beats", 10 * KB + 512, [P, TT, GROUPS, GROUPS])
        ties = place("ties", 11 * KB, [P, TT, GROUPS, GROUPS])
        sh_silu = place("sh_silu", 12 * KB, [P, KF, S])[:]
        sh_t = place("sh_t", 14 * KB, [P, KF, S])[:]

        arena_at = (nc.sbuf_base + 31) // 32 * 32
        arena = sb("arena", [P, 19840])

        def view(at, *shape, dt=F32):
            size = 1
            for n in shape:
                size *= n
            words = size if dt == F32 else size // 2
            v = arena[:, at:at + words]
            if dt != F32:
                v = v.bitcast(dt)
            if len(shape) == 2:
                v = v.rearrange("p (a b) -> p a b", a=shape[0])
            elif len(shape) == 3:
                v = v.rearrange("p (a b c) -> p a b c", a=shape[0], b=shape[1])
            return v

        gu_b = view(0, 2, KD, 2 * FE)
        dn_b = view(8192, 2, KF, D)
        parts = [view(12288 + 1024 * n, TT, KD, P, dt=BF16) for n in range(3)]
        xe_t = view(15360, KD, P)
        y_hi = nc.alloc_sbuf_tensor_at("y_hi", [P, D], F32R, offset=arena_at + 4 * 16384)
        y_lo = nc.alloc_sbuf_tensor_at("y_lo", [P, D], F32R, offset=arena_at + 4 * 18816)
        onehot_t = nc.alloc_sbuf_tensor_at("onehot_t", [P, S], F32R, offset=arena_at + 4 * 17664)
        gates = view(17408, TT, P)
        silu_g = view(17920, FE)
        hid = view(18176, FE)
        hid_t = view(18432, KF, P)
        onehot = view(18688, TT, P, dt=BF16)
        gu = [gu_a[:], gu_b, ring_w[:].rearrange("p e (k n) -> p e k n", k=KD)]
        dn = [dn_a[:], dn_b, dn_c[:]]
        rest = [xe_t, view(16384, KD, P)]

        qa_t, ka_t, va = view(0, KW, S), view(1024, KW, S), view(2048, TT, WIDTH)
        qc_t, kc_t, vc = view(3072, KW, S), view(4096, KW, S), view(5120, TT, WIDTH)
        ub_t = view(6144, KW, S)
        probs = [view(7168, 4, S), view(8192, 4, S)]
        probs_t = view(9216, 4, 2, P)
        ya_t, yc_t, mixed, pooled = view(10240, KW, S), view(11264, KW, S), view(12288, KW, S), view(13312, KW, S)
        bias_rev = view(14336, 8, S)
        yb_t = view(2048, KW, S)
        sig = view(0, KD, S)
        merged = view(3072, KD, S)
        squares, rms = view(7168, KW, S), view(8192, KW, S)
        lam_in = view(12288, L, 4, CHUNK)
        q_t, k_t, v_tok, y_t = [qa_t, qc_t], [ka_t, kc_t], [va, vc], [ya_t, yc_t]
        branch_in = [ya_t, yb_t, yc_t]

        banks = [ctx.enter_context(nc.psum_tensor(f"bank{n}", [P, 512], F32)) for n in range(8)]
        acc = [[banks[2 * t + h] for h in range(2)] for t in range(TT)]
        bank_gather, bank_even, bank_odd, bank_t = banks[4:8]

        def const(name):
            a, b = CONST[name]
            return cst[:, a:b]

        ident = const("ident")

        x_in = [sem(f"x_in{t}") for t in range(TT)]
        const_in = sem("const_in")
        first_in = sem("first_in")
        small_in = sem("small_in")
        params_in = sem("params_in")
        bias_in = sem("bias_in")
        ln_in = sem("ln_in")
        block_in = [sem("block_in0"), sem("block_in1")]
        gu_in = [sem(f"gu_in{n}") for n in range(3)]
        dn_in = [sem(f"dn_in{n}") for n in range(3)]
        out_done = sem("out_done")
        bank_ready = sem("bank_ready")
        bank_free = [sem(f"bank_free{n}") for n in range(RING)]
        setup_done = sem("setup_done")
        setup_pool = sem("setup_pool")
        x_hi_ready = sem("x_hi_ready")
        w_hi_ready = sem("w_hi_ready")
        w_lo_ready = sem("w_lo_ready")
        lam_ready = sem("lam_ready")
        lam_exp = sem("lam_exp")
        bias_masked = sem("bias_masked")
        max_ready = sem("max_ready")
        exp_ready = sem("exp_ready")
        recip_ready = sem("recip_ready")
        scaled = sem("scaled")
        probs_ready = sem("probs_ready")
        rope_ready = sem("rope_ready")
        mixed_ready = sem("mixed_ready")
        squares_ready = sem("squares_ready")
        yc_ready = sem("yc_ready")
        merged_ready = sem("merged_ready")
        h_ready = sem("h_ready")
        var_ready = sem("var_ready")
        std_ready = sem("std_ready")
        ln_done = sem("ln_done")
        sel_ready = sem("sel_ready")
        count_ready = sem("count_ready")
        part_ready = sem("part_ready")
        rest_ready = sem("rest_ready")
        shared_down = sem("shared_down")
        s_ready = sem("s_ready")
        sg_ready = sem("sg_ready")
        gathered = sem("gathered")
        xe_ready = sem("xe_ready")
        up_done = sem("up_done")
        silu_ready = sem("silu_ready")
        hid_ready = sem("hid_ready")
        hid_turned = sem("hid_turned")
        hid_t_ready = sem("hid_t_ready")
        slots_turned = sem("slots_turned")
        gate_s_ready = sem("gate_s_ready")
        onehot_t_ready = sem("onehot_t_ready")
        y_done = sem("y_done")
        y_hi_ready = sem("y_hi_ready")
        y_ready = sem("y_ready")
        combined = sem("combined")
        acc_done = sem("acc_done")
        dve_step = sem("dve_step")
        loads_cleared = sem("loads_cleared")

        def at(l, task):
            n = l * NT + INDEX[task]
            return n, n % RING, n // RING

        def bank(l, task):
            return banks[4 + at(l, task)[1]]

        def wait_task(eng, l, task):
            eng.wait_ge(bank_ready, at(l, task)[0] + 1)

        def wait_evac(eng, l, task):
            _, b, uses = at(l, task)
            eng.wait_ge(bank_free[b], uses + 1)

        def free(ins, l, task):
            ins.then_inc(bank_free[at(l, task)[1]], 1)

        def rounds_of(eng, l):
            eng.wait_ge(count_ready, l + 1)
            most = eng.value_load(count_i[0:1, l:l + 1], min_val=1, max_val=S)
            return eng.snap((most + (SLOTS - 1)) >> 6).with_bounds(min_val=1, max_val=ROUNDS)

        def x_tile(t, j):
            return t[:, 4 * (j % 2):4 * (j % 2) + 4, P * (j // 2):P * (j // 2) + P]

        def z_chunk(u):
            return ring_w[:, BLOCK_OF_Z[u // 2] % 2, :].rearrange("p (k n) -> p k n", k=KD)[
                :, :, S * (u % 2):S * (u % 2) + S]

        HALVES = PAIRS // 2
        PEELED = 4
        PEELED_SLOTS = (0, 1, 2, 0)

        def norm_std(act, l, which, t):
            act.wait_ge(var_ready, TT * (2 * l + which) + t + 1)
            nc.scalar.activation(std[:, t:t + 1], mean_var[:, t, 1:2], ACT.Sqrt,
                                 bias=eps[:, 0:1]).then_inc(std_ready, 1)

        block = ctx.enter_context(nc.Block())

        @block.sync
        def _(sp):
            sp.dma_start(cst[:, 0:P], consts[:, 0:P]).then_inc(x_in[0], 16)
            for t in range(TT):
                sp.dma_start(x_tok[:, t, :], x[0, P * t:P * t + P, :]).then_inc(x_in[t], 16)

            def load_block(l, n):
                kind, b = BLOCKS[n]
                slot, before = n % 2, n - 2
                bl = l if before >= 0 else l - 1
                before %= NB
                if bl >= 0:
                    if BLOCKS[before][0] == "z":
                        sp.wait_ge(w_lo_ready, ZU * bl + 2 * BLOCKS[before][1] + 2)
                    elif before in LAST_OF_BLOCK:
                        wait_task(sp, bl, LAST_OF_BLOCK[before])
                    elif BLOCKS[before][0] == "out":
                        sp.wait_ge(h_ready, 2 * TT * (bl + 1))
                    else:
                        sp.wait_ge(shared_down, bl + 1)
                if kind == "z":
                    c = Z_BLOCKS[b][1]
                    dst = ring_w[:, slot, :].rearrange("p (k n) -> p k n", k=KD)
                    src = w_in[l, :, c:c + WIDTH].rearrange("(p k) n -> p k n", k=KD)
                    if (l, n) == (0, 0):
                        sp.dma_start(dst[:, :, 0:S], src[:, :, 0:S]).then_inc(first_in, 16)
                        sp.dma_start(cst[:, P:], consts[:, P:]).then_inc(const_in, 16)
                        dst, src = dst[:, :, S:], src[:, :, S:]
                elif kind == "branch":
                    dst = ring_w[:, slot, :].rearrange("p (k n) -> p k n", k=KW)
                    src = (w_branch_a, w_branch_b, w_branch_c)[b][l].rearrange("(k p) n -> p k n", p=P)
                elif kind == "out":
                    dst = ring_w[:, slot, :].rearrange("p (k n) -> p k n", k=KD)
                    src = w_out[l, :, 512 * b:512 * b + 512].rearrange("(k p) n -> p k n", p=P)
                elif kind == "shared_up":
                    dst = ring_w[:, slot, :]
                    src = shared_w_gate_up[l].rearrange("(p k) n -> p (k n)", k=KD)
                else:
                    dst = ring_w[:, slot, 0:KF * D].rearrange("p (k n) -> p k n", k=KF)
                    src = shared_w_down[l].rearrange("(k p) n -> p k n", p=P)
                sp.dma_start(dst, src).then_inc(block_in[slot], 16)

            def load_up(l, slot, pair):
                sp.dma_start(gu[slot], expert_w_gate_up[l, bass.ds(2 * pair, 2)]
                             .rearrange("e (p k) n -> p e k n", k=KD)).then_inc(gu_in[slot], 16)

            def load_down(l, slot, pair):
                sp.dma_start(dn[slot], expert_w_down[l, bass.ds(2 * pair, 2)]
                             .rearrange("e (p k) n -> p e k n", k=KF)).then_inc(dn_in[slot], 16)

            def load_after(l, slot, pair, used):
                sp.wait_ge(up_done, used)
                sp.sem_inc(loads_cleared, 1)
                load_up(l, slot, pair)
                sp.wait_ge(y_done, 2 * used)
                sp.sem_inc(loads_cleared, 1)
                load_down(l, slot, pair)

            start = 0
            for l in range(L):
                for n in range(NB - 2):
                    load_block(l, n)
                wait_task(sp, l, ("z", ZU - 1, 0))
                load_up(l, 0, 0)
                load_down(l, 0, 0)
                sp.wait_ge(h_ready, 2 * TT * (l + 1))
                for n in range(NB - 2, NB):
                    load_block(l, n)
                load_up(l, 1, 1)
                load_down(l, 1, 1)
                sp.wait_ge(shared_down, l + 1)
                load_up(l, 2, 2)
                rounds = rounds_of(sp, l)
                load_down(l, 2, 2)
                load_after(l, 0, 3, 2 * start + 1)
                load_after(l, 1, 4, 2 * start + 2)
                load_after(l, 0, 5, 2 * start + 4)
                with sp.Fori(0, rounds * HALVES - 3) as i:
                    pair = 2 * ((i + 3) & (HALVES - 1))
                    for u in range(2):
                        load_after(l, 1 - u, pair + u, 2 * (i + start) + 5 + u)
                start = start + rounds * HALVES
            for t in range(TT):
                sp.wait_ge(ln_done, TT * (2 * L - 1) + t + 1)
                sp.dma_start(out[0, P * t:P * t + P, :], x_tok[:, t, :]).then_inc(out_done, 16)
            sp.wait_ge(out_done, 16 * TT)

        @block.gpsimd
        def _(pool):
            pool.memset(slot_of[:, :, ROUNDS * NE:], -1.0).then_inc(setup_pool, 1)
            pool.memset(gate_of[:, :, ROUNDS * NE:], 0.0).then_inc(setup_pool, 1)

            def split_low(l, u):
                pool.wait_ge(w_hi_ready, ZU * l + u + 1)
                pool.tensor_tensor(w_lo[u % WBUFS][:], z_chunk(u), w_hi[u % WBUFS][:].bitcast(F32),
                                   ALU.subtract).then_inc(w_lo_ready, 1)

            for l in range(L):
                for u in range(WBUFS):
                    split_low(l, u)
                pool.wait_ge(bias_in, 16 * (l + 1))
                pool.memset(bias_rev[0:CHUNK, :, 0:CHUNK], NEG).then_inc(bias_masked, 1)
                for task in PLAN:
                    kind, i, j = task
                    if kind == "z" and i + WBUFS < ZU:
                        split_low(l, i + WBUFS)
                    if kind != "scores" or j == 0:
                        continue
                    g = l * UNITS + i
                    branch, qt, _ = unit(i)
                    W = P * (qt + 1)
                    p = probs[i % 2][:, :, 0:W]
                    pool.wait_ge(recip_ready, g + 1)
                    scale = recips[:, i % 2, :].unsqueeze(2).to_broadcast([P, 4, W])
                    ins = pool.tensor_tensor(p, p, scale, ALU.mult)
                    if branch == 0:
                        ins.then_inc(probs_ready, 1)
                    else:
                        ins.then_inc(scaled, 1)
                        pool.wait_ge(scaled, l * 4 + i - 3)
                        pool.tensor_tensor(p[:, 0::2, :], p[:, 0::2, :], p[:, 1::2, :], ALU.add).then_inc(probs_ready, 1)
                for t in range(TT):
                    for n in range(2):
                        k = 3 * TT * l + 3 * t + n
                        pool.wait_ge(part_ready, k + 1)
                        src = x_tok[:, t, :].rearrange("p (q k) -> p k q", k=KD) if n == 0 else rest[t]
                        if n:
                            pool.wait_ge(rest_ready, 2 * TT * l + 2 * t + n)
                        pool.tensor_tensor(rest[t], src, parts[n][:, t], ALU.subtract).then_inc(rest_ready, 1)

        @block.scalar
        def _(act):
            def load_ln(l, which):
                g, b = ((ln1_g, ln1_b), (ln2_g, ln2_b))[which]
                act.dma_start(ln_gb[:, 0, :], g[l].partition_broadcast(P)).then_inc(ln_in, 16)
                act.dma_start(ln_gb[:, 1, :], b[l].partition_broadcast(P)).then_inc(ln_in, 16)

            def load_bias(l):
                head = 2 * REL_CLIP + 1
                rows = bass.AP(tensor=rel_bias.tensor, offset=rel_bias.offset + l * 8 * head + REL_CLIP - P + 1,
                               ap=[[1, P], [head, 8], [1, S]])
                act.dma_start(bias_rev, rows).then_inc(bias_in, 16)

            def load_params(l):
                act.dma_start(router_sb[:], router_w[l].rearrange("(p k) e -> p k e", k=KD)).then_inc(params_in, 16)
                act.dma_start(pool_w_sb[:], pool_w[l].rearrange("g c d -> c g d")).then_inc(params_in, 16)

            def load_smalls():
                for l in range(L):
                    for n, vec in enumerate((lambda_q1, lambda_k1, lambda_q2, lambda_k2)):
                        act.dma_start(lam_in[:, l, n, :], vec[l].partition_broadcast(P)).then_inc(small_in, 16)
                    act.dma_start(rbias_sb[:, l, :], router_bias[l].partition_broadcast(P)).then_inc(small_in, 16)
                    with nc.allow_non_contiguous_dma(reason="a few hundred words, once"):
                        act.dma_start(pool_s_sb[:, l], pool_scale[l].rearrange("(g p) -> p g", p=P)).then_inc(small_in, 16)
                        act.dma_start(subln_sb[:, l:l + 1], subln_g[l].rearrange("(p a) -> p a", a=1)).then_inc(small_in, 16)

            def split_high(l, u):
                n = BLOCK_OF_Z[u // 2]
                if (l, u) == (0, 0):
                    act.wait_ge(first_in, 16)
                elif u % 2 == 0 or (l, u) == (0, 1):
                    act.wait_ge(block_in[n % 2], 16 * (l * (NB // 2) + n // 2 + 1))
                nc.scalar.copy(w_hi[u % WBUFS][:], z_chunk(u)).then_inc(w_hi_ready, 1)

            start = 0
            for l in range(L):
                for task in PLAN:
                    kind, i, j = task
                    b = bank(l, task)
                    if l == 0 and task == ("z", 2, 0):
                        act.wait_ge(lam_ready, 1)
                        nc.scalar.activation(lam_sum[:], lam_sum[:], ACT.Exp).then_inc(lam_exp, 1)
                    if kind == "xt" and i == 0:
                        wait_task(act, l, task)
                        nc.scalar.copy(x_tile(x_hi, j), b[:].rearrange("p (c n) -> p c n", c=4)).then_inc(x_hi_ready, 1)
                        if j == 3:
                            if l == 0:
                                for u in range(WBUFS):
                                    split_high(0, u)
                                    if u == 0:
                                        load_smalls()
                                        load_bias(0)
                                        load_params(0)
                            else:
                                act.wait_ge(ln_done, TT * 2 * l)
                            load_ln(l, 0)
                    elif kind == "xt" and j % 2 == 0:
                        wait_task(act, l, task)
                        free(nc.scalar.copy(x_tile(x_t, j), b[:].rearrange("p (c n) -> p c n", c=4)), l, task)
                    elif kind == "z":
                        wait_task(act, l, task)
                        name, half = Z_BLOCKS[i // 2][0], i % 2
                        two = b[:].rearrange("p (c n) -> p c n", c=2)
                        if name in ("ga", "gb", "gc"):
                            v = (i - 14) % 4
                            if name != "ga":
                                wait_evac(act, l, ("branch", 0 if name == "gb" else 1, v))
                            ins = nc.scalar.activation(sig[:, 2 * v:2 * v + 2, :], two, ACT.Sigmoid)
                        elif name in ("va", "vc"):
                            ins = nc.scalar.copy((va if name == "va" else vc)[:, :, S * half:S * half + S], two)
                        else:
                            dst = {"qa": qa_t, "ka": ka_t, "qc": qc_t, "kc": kc_t, "ub": ub_t}[name]
                            ins = nc.scalar.copy(dst[:, 2 * half:2 * half + 2, :], two)
                        free(ins, l, task)
                        if i + WBUFS < ZU:
                            split_high(l, i + WBUFS)
                    elif kind == "scores" and j == 1:
                        g, W = l * UNITS + i, P * (unit(i)[1] + 1)
                        act.wait_ge(max_ready, g + 1)
                        for m in range(4):
                            p = probs[i % 2][:, m, 0:W]
                            ins = nc.scalar.activation(p, p, ACT.Exp, bias=neg_max[:, i % 2, m:m + 1],
                                                       accum_out=sums[:, i % 2, m:m + 1])
                        ins.then_inc(exp_ready, 1)
                    elif kind == "turn":
                        wait_task(act, l, task)
                        branch, qt, _ = unit(i)
                        s0 = 2 * j if branch == 0 else 0
                        free(nc.scalar.copy(probs_t[:, s0:s0 + 2, 0:qt + 1, :],
                                            b[:, 0:2 * (qt + 1) * P].rearrange("p (m k n) -> p m k n", m=2, k=qt + 1)),
                             l, task)
                    elif kind == "rms":
                        wait_task(act, l, task)
                        free(nc.scalar.activation(rms[:, 2 * i:2 * i + 2, :], b[:].rearrange("p (c n) -> p c n", c=2),
                                                  ACT.Sqrt, bias=eps[:, 1:2], scale=1.0 / P), l, task)
                    elif kind == "router":
                        wait_task(act, l, task)
                        free(nc.scalar.activation(score[:], b[:, 0:TT * NE].rearrange("p (t e) -> p t e", t=TT),
                                                  ACT.Exp, scale=-1.0), l, task)
                    elif kind == "shared" and i == 0:
                        wait_task(act, l, task)
                        free(nc.scalar.activation(sh_silu, b[:].rearrange("p (c n) -> p c n", c=2), ACT.Silu), l, task)
                    if task == ("branch", 2, 3):
                        for t in range(TT):
                            norm_std(act, l, 0, t)
                    if task == ("xt", 1, 2):
                        act.wait_ge(ln_done, TT * 2 * l + TT)
                        load_ln(l, 1)

                if l + 1 < L:
                    load_params(l + 1)

                for t in range(TT):
                    for n in range(3):
                        src = x_tok[:, t, :].rearrange("p (q k) -> p k q", k=KD) if n == 0 else rest[t]
                        if n:
                            act.wait_ge(rest_ready, 2 * TT * l + 2 * t + n)
                        nc.scalar.copy(parts[n][:, t], src).then_inc(part_ready, 1)

                def gather_out(n, half):
                    act.wait_ge(gathered, 2 * (n + l) + half + 1)
                    nc.scalar.copy(xe_t[:, 4 * half:4 * half + 4, :],
                                   bank_gather[:].rearrange("p (c n) -> p c n", c=4)).then_inc(xe_ready, 1)

                def pair_step(n, odd):
                    bank_up, bank_other = (bank_even, bank_odd)[::-1 if odd else 1]
                    act.wait_ge(up_done, n + 1)
                    nc.scalar.activation(silu_g, bank_up[:, 0:FE], ACT.Silu).then_inc(silu_ready, 1)
                    for h in range(2):
                        act.wait_ge(y_done, 2 * n + h + 1)
                        nc.scalar.copy(y_hi[:, 512 * h:512 * h + 512], (bank_other, bank_up)[h][:]).then_inc(y_hi_ready, 1)
                        gather_out(n + 1, h)

                rounds = rounds_of(act, l)
                gather_out(2 * start, 0)
                gather_out(2 * start, 1)
                for n in range(PEELED):
                    pair_step(2 * start + n, n % 2)
                with act.Fori(0, rounds * HALVES - 2) as i:
                    for u in range(2):
                        pair_step(2 * (i + start) + PEELED + u, u)
                start = start + rounds * HALVES
                if l + 1 < L:
                    act.wait_ge(y_done, 4 * start)
                    split_high(l + 1, 0)
                for t in range(TT):
                    norm_std(act, l, 1, t)
                    if l + 1 < L:
                        split_high(l + 1, t + 1)
                if l + 1 < L:
                    act.wait_ge(xe_ready, 2 * (2 * start + l) + 2)
                    act.sem_inc(loads_cleared, 1)
                    load_bias(l + 1)

        @block.vector
        def _(dve):
            steps = [0]

            def step(ins):
                ins.then_inc(dve_step, 1)
                steps[0] += 1

            def settle():
                dve.wait_ge(dve_step, steps[0])

            v = nc.vector
            dve.wait_ge(x_in[0], 32)
            dve.wait_ge(const_in, 16)
            v.tensor_copy(before_b[:], const("before")).then_inc(setup_done, 1)
            v.tensor_copy(ones_b[:], const("ones")).then_inc(setup_done, 1)
            v.tensor_copy(ident_b[:], ident).then_inc(setup_done, 1)
            v.memset(eps[:, 0:1], LN_EPS).then_inc(setup_done, 1)
            v.memset(eps[:, 1:2], RMS_EPS).then_inc(setup_done, 1)
            def lambdas():
                dve.wait_ge(small_in, 16 * 7 * L)
                for l in range(L):
                    step(v.tensor_tensor(lam_in[:, l, 0::2, :], lam_in[:, l, 0::2, :], lam_in[:, l, 1::2, :], ALU.mult))
                    step(v.tensor_scalar(subln_sb[:, l:l + 1], subln_sb[:, l:l + 1], 1.0 - lambda_init[l], None, ALU.mult))
                settle()
                for l in range(L):
                    ins = v.tensor_reduce(lam_sum[:, l, :], lam_in[:, l, 0::2, :], AX, ALU.add)
                    if l < L - 1:
                        step(ins)
                ins.then_inc(lam_ready, 1)
                dve.wait_ge(lam_exp, 1)
                step(v.tensor_tensor(nlam[:], lam_sum[:, :, 1], lam_sum[:, :, 0], ALU.subtract))
                settle()
                for l in range(L):
                    step(v.tensor_scalar(nlam[:, l:l + 1], nlam[:, l:l + 1], -lambda_init[l], None, ALU.add))

            def norm(l, which):
                k = 2 * l + which
                dve.wait_ge(ln_in, 32 * (k + 1))
                for t in range(TT):
                    row = x_tok[:, t, :]
                    for h in range(2):
                        if which == 0:
                            dve.wait_ge(h_ready, 2 * TT * l + 2 * t + h + 1)
                        else:
                            dve.wait_ge(acc_done, 2 * TT * l + TT * h + t + 1)
                        part = x_tok[:, t, 512 * h:512 * h + 512]
                        step(v.scalar_tensor_tensor(out=part, in0=part, scalar=ALPHA, in1=acc[t][h][:],
                                                    op0=ALU.mult, op1=ALU.add))
                        settle()
                        step(v.bn_stats(stats[:, h, :], part))
                    settle()
                    v.bn_aggr(mean_var[:, t, :], stats[:].rearrange("p a b -> p (a b)")).then_inc(var_ready, 1)
                    dve.wait_ge(var_ready, TT * k + t + 1)
                    step(v.scalar_tensor_tensor(out=row, in0=row, scalar=mean_var[:, t, 0:1], in1=ln_gb[:, 0, :],
                                                op0=ALU.subtract, op1=ALU.mult))
                    dve.wait_ge(std_ready, TT * k + t + 1)
                    step(v.reciprocal(rstd[:, t:t + 1], std[:, t:t + 1]))
                    settle()
                    v.scalar_tensor_tensor(out=row, in0=row, scalar=rstd[:, t:t + 1], in1=ln_gb[:, 1, :],
                                           op0=ALU.mult, op1=ALU.add).then_inc(ln_done, 1)

            def pool_windows(l):
                wait_evac(dve, l, ("z", 12, 0))
                wait_evac(dve, l, ("z", 13, 0))
                dve.wait_ge(rope_ready, 4 * (l + 1))
                src, dst, other = ub_t, mixed, pooled
                for level in range(4):
                    n = 1 << level
                    g = slice(level, KW)
                    step(v.tensor_tensor(dst[:, g, n:], src[:, g, n:], src[:, g, :S - n], ALU.add))
                    step(v.tensor_copy(dst[:, g, 0:n], src[:, g, 0:n]))
                    settle()
                    src, dst, other = dst, other, dst
                for g, w in enumerate(POOL_WINDOWS):
                    s = (mixed, pooled)[g % 2]
                    ramp = const("ramp")[:, 16 * g:16 * g + 16]
                    step(v.tensor_tensor(s[:, g, 0:16], s[:, g, 0:16], ramp, ALU.mult))
                settle()
                for g, w in enumerate(POOL_WINDOWS):
                    s = (mixed, pooled)[g % 2]
                    ins = v.scalar_tensor_tensor(out=mixed[:, g, :], in0=s[:, g, :], scalar=1.0 / w, in1=ub_t[:, g, :],
                                                 op0=ALU.mult, op1=ALU.subtract)
                    if g < KW - 1:
                        step(ins)
                ins.then_inc(mixed_ready, 1)

            def route(l):
                wait_evac(dve, l, ("router", 0, 0))
                step(v.tensor_scalar(score[:], score[:], 1.0, None, ALU.add))
                settle()
                step(v.reciprocal(score[:], score[:]))
                settle()
                step(v.tensor_tensor(choice[:], score[:], rbias_sb[:, l, :].unsqueeze(1).to_broadcast([P, TT, NE]),
                                     ALU.add))
                settle()
                for t in range(TT):
                    for g in range(GROUPS):
                        step(v.max(top[:, t * GROUPS + g, :], choice[:, t, 8 * g:8 * g + 8]))
                settle()
                step(v.tensor_tensor(group_s[:].rearrange("p t g -> p (t g)"), top[:, :, 0], top[:, :, 1], ALU.add))
                settle()
                one = group_s[:].unsqueeze(3).to_broadcast([P, TT, GROUPS, GROUPS])
                other = group_s[:].unsqueeze(2).to_broadcast([P, TT, GROUPS, GROUPS])
                earlier = const("earlier").unsqueeze(1).to_broadcast([P, TT, GROUPS * GROUPS])
                step(v.tensor_tensor(beats[:], other, one, ALU.is_gt))
                step(v.tensor_tensor(ties[:], other, one, ALU.is_equal))
                settle()
                flat = ties[:].rearrange("p t a b -> p t (a b)")
                step(v.tensor_tensor(flat, flat, earlier, ALU.mult))
                settle()
                step(v.tensor_tensor(beats[:], beats[:], ties[:], ALU.add))
                settle()
                step(v.tensor_reduce(group_r[:], beats[:], AX, ALU.add))
                settle()
                step(v.tensor_scalar(group_r[:], group_r[:], TOPK_GROUPS - 0.5, NEG, ALU.is_gt, ALU.mult))
                settle()
                by_group = choice[:].rearrange("p t (g e) -> p (t g) e", g=GROUPS)
                out_of = group_r[:].rearrange("p t g -> p (t g)").unsqueeze(2).to_broadcast([P, TT * GROUPS, 8])
                step(v.tensor_tensor(by_group, by_group, out_of, ALU.add))
                settle()
                for t in range(TT):
                    step(v.max(top[:, t, :], choice[:, t, :]))
                settle()
                for t in range(TT):
                    step(v.match_replace(out=replaced[:, t, :], in_to_replace=top[:, t, :], in_values=choice[:, t, :],
                                         imm_value=3 * NEG))
                settle()
                v.tensor_tensor(sel_b[:], replaced[:], choice[:], ALU.not_equal).then_inc(sel_ready, 1)
                step(v.tensor_tensor(sel[:], replaced[:], choice[:], ALU.not_equal))
                settle()
                step(v.tensor_tensor(score[:], score[:], sel[:], ALU.mult))
                settle()
                step(v.tensor_reduce(wsum[:], score[:], AX, ALU.add))
                settle()
                step(v.reciprocal(wsum[:], wsum[:]))
                settle()
                for t in range(TT):
                    step(v.tensor_scalar(gate_of[:, t, 0:NE], score[:, t, :], wsum[:, t:t + 1], ROUTED_SCALE,
                                         ALU.mult, ALU.mult))
                settle()
                for r in range(1, ROUNDS):
                    step(v.tensor_copy(gate_of[:, :, r * NE:(r + 1) * NE], gate_of[:, :, 0:NE]))
                step(v.tensor_scalar(choice[:], sel[:], 1000.0, -1000.0, ALU.mult, ALU.add))
                settle()

            def ranks(l):
                task = ("rank", 0, 0)
                b = bank(l, task)
                wait_task(dve, l, task)
                step(v.tensor_tensor(slot_of[:, :, 0:NE], b[:, 0:TT * NE].rearrange("p (t e) -> p t e", t=TT), sel[:],
                                     ALU.mult))
                free(v.tensor_reduce(count_f[:], b[:, TT * NE:(TT + 1) * NE], AX, ALU.max), l, task)
                settle()
                step(v.tensor_tensor(slot_of[:, :, 0:NE], slot_of[:, :, 0:NE], choice[:], ALU.add))
                settle()
                wait_evac(dve, l, task)
                v.tensor_copy(count_i[:, l:l + 1], count_f[:]).then_inc(count_ready, 1)
                for r in range(1, ROUNDS):
                    step(v.tensor_scalar(slot_of[:, :, r * NE:(r + 1) * NE], slot_of[:, :, 0:NE], float(-SLOTS * r), None,
                                         ALU.add))
                settle()

            def slots(n, l, col):
                iota = const("iota").unsqueeze(1).unsqueeze(1).to_broadcast([P, TT, 2, SLOTS])
                rank = slot_of[:, :, bass.ds(col, 2)].unsqueeze(3).to_broadcast([P, TT, 2, SLOTS])
                gate = gate_of[:, :, bass.ds(col, 2)].unsqueeze(3).to_broadcast([P, TT, 2, SLOTS])
                hot = onehot.rearrange("p t (e c) -> p t e c", e=2)
                if not isinstance(n, int) or n + l:
                    dve.wait_ge(sg_ready, n + l)
                v.tensor_tensor(hot, rank, iota, ALU.is_equal).then_inc(s_ready, 1)
                dve.wait_ge(s_ready, n + l + 1)
                v.tensor_tensor(gates.rearrange("p t (e c) -> p t e c", e=2), hot, gate, ALU.mult).then_inc(sg_ready, 1)

            start = 0
            for l in range(L):
                for task in PLAN:
                    kind, i, j = task
                    b = bank(l, task)
                    pair = b[:].rearrange("p (c n) -> p c n", c=2)
                    if kind == "xt" and i == 0:
                        dve.wait_ge(x_hi_ready, 4 * l + j + 1)
                        free(v.tensor_tensor(x_tile(x_lo, j), b[:].rearrange("p (c n) -> p c n", c=4),
                                             x_tile(x_hi, j).bitcast(F32), ALU.subtract), l, task)
                        if (l, j) == (0, 3):
                            lambdas()
                    elif kind == "xt" and j % 2 == 1:
                        wait_task(dve, l, task)
                        free(v.tensor_copy(x_tile(x_t, j), b[:].rearrange("p (c n) -> p c n", c=4)), l, task)
                    elif kind == "scores":
                        branch, qt, g = unit(i)
                        W = P * (qt + 1)
                        wait_task(dve, l, task)
                        if i >= 2:
                            wait_task(dve, l, ("turn", i - 2, 1 if unit(i - 2)[0] == 0 else 0))
                        if branch == 0:
                            if (i, j) == (0, 0):
                                dve.wait_ge(bias_masked, l + 1)
                            m = 4 * g + j
                            add = bias_rev[:, m:m + 3:2, 0:W][:, :, ::-1]
                        else:
                            add = const("mask")[:, S - W:S].unsqueeze(1).to_broadcast([P, 2, W])
                        free(v.scalar_tensor_tensor(out=probs[i % 2][:, j::2, 0:W],
                                                    in0=b[:, 0:2 * W].rearrange("p (m n) -> p m n", m=2),
                                                    scalar=float(CHUNK) ** -0.5, in1=add, op0=ALU.mult, op1=ALU.add),
                             l, task)
                        if j == 1:
                            wait_evac(dve, l, ("scores", i, 0))
                            wait_evac(dve, l, task)
                            v.tensor_reduce(neg_max[:, i % 2, :], probs[i % 2][:, :, 0:W], AX, ALU.max,
                                            negate=True).then_inc(max_ready, 1)
                            dve.wait_ge(exp_ready, l * UNITS + i + 1)
                            ins = v.reciprocal(recips[:, i % 2, :], sums[:, i % 2, :])
                            if branch == 1:
                                step(ins)
                                settle()
                                odd = recips[:, i % 2, 1::2]
                                ins = v.tensor_scalar(odd, odd, nlam[:, l:l + 1], None, ALU.mult)
                            ins.then_inc(recip_ready, 1)
                    elif kind == "pv":
                        branch, qt, g = unit(i)
                        wait_task(dve, l, task)
                        free(v.tensor_copy(y_t[branch][:, 2 * g:2 * g + 2, P * qt:P * qt + P],
                                           b[:, 0:2 * P].rearrange("p (c n) -> p c n", c=2)), l, task)
                        if i == 7:
                            for k in range(4, 8):
                                wait_evac(dve, l, ("pv", k, 0))
                            v.tensor_tensor(squares, yc_t, yc_t, ALU.mult).then_inc(squares_ready, 1)
                    elif kind == "rope":
                        raw = (qc_t, kc_t)[i][:, 2 * j:2 * j + 2, :]
                        wait_task(dve, l, task)
                        if 4 * l + 2 * i + j:
                            dve.wait_ge(rope_ready, 4 * l + 2 * i + j)
                        turned = pooled[:, 0:2, :]
                        plain = pooled[:, 2:4, :]
                        free(v.tensor_tensor(turned, pair, const("sin").unsqueeze(1).to_broadcast([P, 2, S]), ALU.mult),
                             l, task)
                        step(v.tensor_tensor(plain, raw, const("cos").unsqueeze(1).to_broadcast([P, 2, S]), ALU.mult))
                        settle()
                        wait_evac(dve, l, task)
                        v.tensor_tensor(raw, plain, turned, ALU.add).then_inc(rope_ready, 1)
                    elif kind == "pool":
                        wait_task(dve, l, task)
                        for c in range(2):
                            g = 2 * i + c
                            ins = v.tensor_scalar(yb_t[:, g, :], b[:, S * c:S * c + S], pool_s_sb[:, l, g:g + 1], None,
                                                  ALU.mult)
                        free(ins, l, task)
                    elif kind == "rms":
                        wait_evac(dve, l, task)
                        r, y = rms[:, 2 * i:2 * i + 2, :], yc_t[:, 2 * i:2 * i + 2, :]
                        step(v.reciprocal(r, r))
                        settle()
                        v.scalar_tensor_tensor(out=y, in0=y, scalar=subln_sb[:, l:l + 1], in1=r, op0=ALU.mult,
                                               op1=ALU.mult).then_inc(yc_ready, 1)
                    elif kind == "branch":
                        wait_task(dve, l, task)
                        wait_evac(dve, l, ("z", 14 + 4 * i + j, 0))
                        if i:
                            settle()
                        s, m = sig[:, 2 * j:2 * j + 2, :], merged[:, 2 * j:2 * j + 2, :]
                        if i == 0:
                            free(v.tensor_tensor(m, pair, s, ALU.mult), l, task)
                        else:
                            add = pooled[:, 2 * (j % 2):2 * (j % 2) + 2, :]
                            if i == 2 and j >= 2:
                                dve.wait_ge(merged_ready, 4 * l + j - 1)
                            free(v.tensor_tensor(add, pair, s, ALU.mult), l, task)
                            wait_evac(dve, l, task)
                            if i == 1:
                                wait_evac(dve, l, ("branch", 0, j))
                            ins = v.tensor_tensor(m, m, add, ALU.add)
                            if i == 1:
                                step(ins)
                            else:
                                ins.then_inc(merged_ready, 1)
                    elif kind == "shared" and i == 1:
                        wait_task(dve, l, task)
                        wait_evac(dve, l, ("shared", 0, 0))
                        free(v.tensor_tensor(sh_t, sh_silu, pair, ALU.mult), l, task)
                    if task == ("pv", 5, 0):
                        pool_windows(l)
                    if task == ("branch", 2, 3):
                        norm(l, 0)
                    if task == ("router", 0, 0):
                        route(l)
                    if task == ("rank", 0, 0):
                        ranks(l)

                dve.wait_ge(setup_pool, 2)
                slots(2 * start, l, 0)
                rounds = rounds_of(dve, l)

                def pair_step(n, col, odd, combined_before):
                    bank_up, bank_other = (bank_even, bank_odd)[::-1 if odd else 1]
                    dve.wait_ge(slots_turned, n + 1)
                    v.tensor_copy(gate_s[:], bank_t[:, 0:1]).then_inc(gate_s_ready, 1)
                    slots(n + 1, l, col + 2)
                    dve.wait_ge(gate_s_ready, n + 1)
                    dve.wait_ge(silu_ready, n + 1)
                    v.scalar_tensor_tensor(out=hid, in0=silu_g, scalar=gate_s[:, 0:1], in1=bank_up[:, FE:2 * FE],
                                           op0=ALU.mult, op1=ALU.mult).then_inc(hid_ready, 1)
                    dve.wait_ge(hid_turned, n + 1)
                    v.tensor_copy(hid_t, bank_t[:, 0:FE].rearrange("p (k n) -> p k n", k=KF)).then_inc(hid_t_ready, 1)
                    if combined_before is not None:
                        dve.wait_ge(combined, combined_before)
                    v.tensor_copy(onehot_t[:], bank_t[:, FE:FE + S]).then_inc(onehot_t_ready, 1)
                    for h in range(2):
                        dve.wait_ge(y_hi_ready, 2 * n + h + 1)
                        part = slice(512 * h, 512 * h + 512)
                        v.tensor_tensor(y_lo[:, part], (bank_other, bank_up)[h][:], y_hi[:, part].bitcast(F32),
                                        ALU.subtract).then_inc(y_ready, 1)

                for n in range(PEELED):
                    pair_step(2 * start + n, 2 * n, n % 2, 2 * start - l + n if n else None)
                with dve.Fori(0, rounds * HALVES - 2) as i:
                    for u in range(2):
                        pair_step(2 * (i + start) + PEELED + u, 4 * i + 2 * (PEELED + u), u,
                                  2 * (i + start) + PEELED + u - l)
                start = start + rounds * HALVES
                norm(l, 1)

        @block.tensor
        def _(pe):
            mm = nc.tensor.matmul
            def acquire(l, task):
                n, b, uses = at(l, task)
                if uses:
                    pe.wait_ge(bank_free[b], uses)

            def block_ready(l, n):
                pe.wait_ge(block_in[n % 2], 16 * (l * (NB // 2) + n // 2 + 1))

            def slot_of_block(n, k):
                return ring_w[:, n % 2, :].rearrange("p (k n) -> p k n", k=k)

            start = 0
            for l in range(L):
                for task in PLAN:
                    kind, i, j = task
                    if task == ("xt", 1, 0):
                        pe.wait_ge(merged_ready, 4 * (l + 1))
                        for t in range(TT):
                            for h in range(2):
                                n = BLOCK_OF["out", h]
                                if t == 0:
                                    block_ready(l, n)
                                for k in range(KD):
                                    ins = mm(acc[t][h][:], merged[:, k, P * t:P * t + P], slot_of_block(n, KD)[:, k, :],
                                             start=(k == 0), stop=(k == KD - 1))
                                ins.then_inc(h_ready, 1)
                    if kind == "rank":
                        n = BLOCK_OF["shared_down", 0]
                        block_ready(l, n)
                        wait_evac(pe, l, ("shared", 1, 0))
                        for t in range(TT):
                            for h in range(2):
                                for k in range(KF):
                                    ins = mm(acc[t][h][:], sh_t[:, k, P * t:P * t + P],
                                             ring_w[:, n % 2, D * k + 512 * h:D * k + 512 * h + 512],
                                             start=(k == 0), stop=(k == KF - 1))
                        ins.then_inc(shared_down, 1)
                    acquire(l, task)
                    b = bank(l, task)
                    if kind == "xt":
                        t = j // 2
                        if i == 0 and l == 0:
                            pe.wait_ge(x_in[t], 32 if t == 0 else 16)
                        else:
                            pe.wait_ge(ln_done, TT * (2 * l - 1 + i) + t + 1)
                        for c in range(4):
                            ins = nc.tensor.transpose(b[:, P * c:P * c + P], x_tok[:, t, 4 * (j % 2) + c::KD], ident)
                    elif kind == "z":
                        if i == 0:
                            for g in range(4):
                                wait_evac(pe, l, ("xt", 0, g))
                        pe.wait_ge(w_lo_ready, ZU * l + i + 1)
                        hi, lo = w_hi[i % WBUFS], w_lo[i % WBUFS]
                        by_token = Z_BLOCKS[i // 2][0] in ("va", "vc")
                        for c in range(2):
                            cols = slice(P * c, P * c + P)
                            for k in range(KD):
                                for a, w in ((0, 0), (0, 1), (1, 0)):
                                    wk, xk = (hi, lo)[a][:, k, :], (x_hi, x_lo)[w][:, k, :]
                                    if by_token:
                                        lhs, rhs = (x_hi, x_lo)[a][:, k, cols], (hi, lo)[w][:, k, :]
                                    else:
                                        lhs, rhs = wk[:, cols], xk
                                    ins = mm(b[:, S * c:S * c + S], lhs, rhs, start=(k == 0 and a + w == 0),
                                             stop=(k == KD - 1 and a == 1))
                    elif kind == "scores":
                        branch, qt, g = unit(i)
                        W = P * (qt + 1)
                        if branch == 0 and i == 0 and j == 0:
                            for u in range(4):
                                wait_evac(pe, l, ("z", u, 0))
                        if branch == 1:
                            pe.wait_ge(rope_ready, 4 * (l + 1))
                        rows = slice(CHUNK * j, CHUNK * j + CHUNK)
                        for m in range(2):
                            ins = mm(b[:, W * m:W * m + W], q_t[branch][rows, 2 * g + m, P * qt:P * qt + P],
                                     k_t[branch][rows, 2 * g + m, 0:W], start=True, stop=True)
                    elif kind == "turn":
                        branch, qt, g = unit(i)
                        pe.wait_ge(probs_ready, l * UNITS + i + 1)
                        maps = (2 * j, 2 * j + 1) if branch == 0 else (0, 2)
                        for n, m in enumerate(maps):
                            for kt in range(qt + 1):
                                c = P * (n * (qt + 1) + kt)
                                ins = nc.tensor.transpose(b[:, c:c + P], probs[i % 2][:, m, P * kt:P * kt + P], ident)
                    elif kind == "pv":
                        branch, qt, g = unit(i)
                        for k in range(2 if branch == 0 else 1):
                            wait_evac(pe, l, ("turn", i, k))
                        if i in (0, 4):
                            first = 4 if branch == 0 else 10
                            wait_evac(pe, l, ("z", first, 0))
                            wait_evac(pe, l, ("z", first + 1, 0))
                        for m in range(4 if branch == 0 else 2):
                            for kt in range(qt + 1):
                                if branch == 0:
                                    o = b[CHUNK * (m % 2):CHUNK * (m % 2) + CHUNK, P * (m // 2):P * (m // 2) + P]
                                    val = va[:, kt, CHUNK * (4 * g + m):CHUNK * (4 * g + m) + CHUNK]
                                else:
                                    o = b[:, P * m:P * m + P]
                                    val = vc[:, kt, P * (2 * g + m):P * (2 * g + m) + P]
                                ins = mm(o, val, probs_t[:, m, kt, :], start=(kt == 0), stop=(kt == qt))
                    elif kind == "rope":
                        wait_evac(pe, l, ("z", (6, 8)[i] + j, 0))
                        if l == 0:
                            pe.wait_ge(const_in, 16)
                        for c in range(2):
                            ins = mm(b[:, S * c:S * c + S], const("rotate"), (qc_t, kc_t)[i][:, 2 * j + c, :],
                                     start=True, stop=True)
                    elif kind == "pool":
                        pe.wait_ge(mixed_ready, l + 1)
                        pe.wait_ge(params_in, 32 * (l + 1))
                        for c in range(2):
                            g = 2 * i + c
                            ins = mm(b[:, S * c:S * c + S], pool_w_sb[:, g, :], mixed[:, g, :], start=True, stop=True)
                    elif kind == "rms":
                        pe.wait_ge(squares_ready, l + 1)
                        for c in range(2):
                            ins = mm(b[:, S * c:S * c + S], const("ones"), squares[:, 2 * i + c, :], start=True, stop=True)
                    elif kind == "branch":
                        n = BLOCK_OF["branch", i]
                        if j == 0:
                            block_ready(l, n)
                            if i == 0:
                                for k in range(4):
                                    wait_evac(pe, l, ("pv", k, 0))
                            elif i == 1:
                                wait_evac(pe, l, ("pool", 0, 0))
                                wait_evac(pe, l, ("pool", 1, 0))
                            else:
                                pe.wait_ge(yc_ready, 2 * (l + 1))
                        w = slot_of_block(n, KW)
                        for c in range(2):
                            col = P * (2 * j + c)
                            for k in range(KW):
                                ins = mm(b[:, S * c:S * c + S], w[:, k, col:col + P], branch_in[i][:, k, :],
                                         start=(k == 0), stop=(k == KW - 1))
                    elif kind == "router":
                        for g in range(4):
                            wait_evac(pe, l, ("xt", 1, g))
                        for t in range(TT):
                            for k in range(KD):
                                ins = mm(b[:, NE * t:NE * t + NE], x_t[:, k, P * t:P * t + P], router_sb[:, k, :],
                                         start=(k == 0), stop=(k == KD - 1))
                    elif kind == "shared":
                        n = BLOCK_OF["shared_up", 0]
                        if i == 0:
                            block_ready(l, n)
                        for c in range(2):
                            col = FE * i + P * c
                            for k in range(KD):
                                ins = mm(b[:, S * c:S * c + S], slot_of_block(n, KD)[:, k, col:col + P], x_t[:, k, :],
                                         start=(k == 0), stop=(k == KD - 1))
                    elif kind == "rank":
                        pe.wait_ge(sel_ready, l + 1)
                        if l == 0:
                            pe.wait_ge(setup_done, 5)
                        mm(b[:, 0:NE], before_b[:], sel_b[:, 0, :], start=True, stop=True)
                        mm(b[:, NE:2 * NE], ones_b[:], sel_b[:, 0, :], start=True, stop=False)
                        mm(b[:, NE:2 * NE], before_b[:], sel_b[:, 1, :], start=False, stop=True)
                        mm(b[:, 2 * NE:3 * NE], ones_b[:], sel_b[:, 0, :], start=True, stop=False)
                        ins = mm(b[:, 2 * NE:3 * NE], ones_b[:], sel_b[:, 1, :], start=False, stop=True)
                    ins.then_inc(bank_ready, 1)

                def gather(n, half):
                    for c in range(4):
                        k = 4 * half + c
                        for t in range(TT):
                            for part in range(3):
                                ins = mm(bank_gather[:, P * c:P * c + P], parts[part][:, t, k, :], onehot[:, t, :],
                                         start=(t == 0 and part == 0), stop=(t == TT - 1 and part == 2))
                    ins.then_inc(gathered, 1)

                def combine(half, last=False):
                    for t in range(TT):
                        for part in (y_hi, y_lo):
                            ins = mm(acc[t][half][:], onehot_t[:, P * t:P * t + P], part[:, 512 * half:512 * half + 512],
                                     start=False, stop=True, skip_group_check=True)
                        if last:
                            ins.then_inc(acc_done, 1)
                    return ins

                def pair_step(n, first, odd, slot, loads):
                    bank_up, bank_other = (bank_even, bank_odd)[::-1 if odd else 1]
                    pe.wait_ge(sg_ready, n + l + 1)
                    if not first:
                        pe.wait_ge(onehot_t_ready, n)
                    for t in range(TT):
                        mm(bank_t[:, 0:1], gates[:, t, :], const("ones")[:, 0:1], start=(t == 0), stop=(t == TT - 1))
                    for t in range(TT):
                        ins = mm(bank_t[:, FE + P * t:FE + P * t + P], onehot[:, t, :], ident_b[:], start=True, stop=True)
                    ins.then_inc(slots_turned, 1)
                    pe.wait_ge(gu_in[slot], 16 * loads)
                    if not first:
                        pe.wait_ge(y_ready, 2 * n - 1)
                    for k in range(KD):
                        if k % 4 == 0:
                            pe.wait_ge(xe_ready, 2 * (n + l) + k // 4 + 1)
                        for e in range(2):
                            ins = mm(bank_up[SLOTS * e:SLOTS * e + SLOTS, :], xe_t[:, k, SLOTS * e:SLOTS * e + SLOTS],
                                     gu[slot][:, e, k, :], start=(k == 0), stop=(k == KD - 1))
                    ins.then_inc(up_done, 1)
                    if not first:
                        pe.wait_ge(y_ready, 2 * n)
                        combine(0)
                    pe.wait_ge(hid_ready, n + 1)
                    for k in range(KF):
                        ins = nc.tensor.transpose(bank_t[:, P * k:P * k + P], hid[:, k::KF], ident)
                    ins.then_inc(hid_turned, 1)
                    if not first:
                        combine(1).then_inc(combined, 1)
                    pe.wait_ge(hid_t_ready, n + 1)
                    pe.wait_ge(dn_in[slot], 16 * loads)
                    for h in range(2):
                        for k in range(KF):
                            for e in range(2):
                                ins = mm((bank_other, bank_up)[h][SLOTS * e:SLOTS * e + SLOTS, :],
                                         hid_t[:, k, SLOTS * e:SLOTS * e + SLOTS],
                                         dn[slot][:, e, k, 512 * h:512 * h + 512], start=(k == 0), stop=(k == KF - 1))
                        ins.then_inc(y_done, 1)
                        if h == 0:
                            pe.wait_ge(s_ready, n + l + 2)
                        else:
                            pe.wait_ge(xe_ready, 2 * (n + 1 + l) + 1)
                        gather(n + 1, h)

                rounds = rounds_of(pe, l)
                for task in PLAN[-RING:]:
                    wait_evac(pe, l, task)
                pe.wait_ge(part_ready, 3 * TT * (l + 1))
                pe.wait_ge(s_ready, 2 * start + l + 1)
                gather(2 * start, 0)
                pe.wait_ge(xe_ready, 2 * (2 * start + l) + 1)
                gather(2 * start, 1)
                for n in range(PEELED):
                    slot = PEELED_SLOTS[n]
                    loads = (start + 1, start + 1 - l, l + 1, start + 2)[n]
                    pair_step(2 * start + n, n == 0, n % 2, slot, loads)
                with pe.Fori(0, rounds * HALVES - 2) as i:
                    for u in range(2):
                        loads = i + start + (2 - l, 3)[u]
                        pair_step(2 * (i + start) + PEELED + u, False, u, 1 - u, loads)
                start = start + rounds * HALVES
                pe.wait_ge(onehot_t_ready, 2 * start)
                pe.wait_ge(y_ready, 4 * start)
                combine(0, last=True)
                combine(1, last=True)
                pe.wait_ge(xe_ready, 2 * (2 * start + l) + 2)


def _constants():
    import numpy as np

    c = np.zeros((P, CONST_COLS), np.float32)

    def put(name, value):
        a, b = CONST[name]
        c[:, a:b] = value

    p = np.arange(P)
    half = ROPE_DIM // 2
    inv = np.float32(ROPE_THETA) ** (-np.arange(0, ROPE_DIM, 2, dtype=np.float32) / np.float32(ROPE_DIM))
    ang = np.arange(S, dtype=np.float32)[:, None] * inv[None, :].astype(np.float32)
    cos, sin = np.ones((P, S), np.float32), np.zeros((P, S), np.float32)
    rotate = np.zeros((P, P), np.float32)
    for base in (0, CHUNK):
        for n in range(half):
            for at in (base + n, base + half + n):
                cos[at], sin[at] = np.cos(ang[:, n]), np.sin(ang[:, n])
            rotate[base + half + n, base + n] = -1.0
            rotate[base + n, base + half + n] = 1.0
    put("cos", cos)
    put("sin", sin)
    put("rotate", rotate)
    put("ident", np.eye(P, dtype=np.float32))
    mask = np.zeros((P, S), np.float32)
    mask[:CHUNK, S - CHUNK:] = NEG
    put("mask", mask)
    put("iota", np.arange(SLOTS, dtype=np.float32)[None, :])
    g = np.arange(GROUPS)
    put("earlier", (g[None, :] < g[:, None]).astype(np.float32).reshape(1, -1))
    put("before", (p[:, None] < p[None, :]).astype(np.float32))
    put("ones", 1.0)
    t = np.arange(16)
    put("ramp", np.concatenate([w / np.minimum(t + 1, w) for w in POOL_WINDOWS]).astype(np.float32)[None, :])
    return c


_INS = ["x", "w_in", "rel_bias", "pool_w", "pool_scale", "lambda_q1", "lambda_k1", "lambda_q2", "lambda_k2",
        "subln_g", "w_branch_a", "w_branch_b", "w_branch_c", "w_out", "ln1_g", "ln1_b", "router_w", "router_bias",
        "expert_w_gate_up", "expert_w_down", "shared_w_gate_up", "shared_w_down", "ln2_g", "ln2_b"]


def kernel(**inputs):
    import numpy as _np
    import concourse.bacc as _bacc
    from concourse import mybir as _mybir
    from concourse.bass_utils import run_bass_kernel_spmd as _run

    nc = _bacc.Bacc("TRN2", target_bir_lowering=False, num_devices=1)
    arrays, args = {}, []
    for name in _INS:
        a = _np.ascontiguousarray(inputs[name])
        arrays[f"in_{name}"] = a
        args.append(nc.dram_tensor(f"in_{name}", a.shape, _mybir.dt.from_np(a.dtype), kind="ExternalInput").ap())
    table = _constants()
    arrays["in_consts"] = table
    args.append(nc.dram_tensor("in_consts", table.shape, _mybir.dt.from_np(table.dtype), kind="ExternalInput").ap())
    args.append([0.8 - 0.6 * float(_np.exp(-0.3 * l)) for l in range(L)])
    args.append(nc.dram_tensor("out_0", (1, S, D), _mybir.dt.float32, kind="ExternalOutput").ap())
    build(nc, *args)
    r = _run(nc, [arrays], core_ids=[0])
    return r.results[0]["out_0"]
```

```python
from contextlib import ExitStack

import concourse.bass as bass
from concourse import mybir

F32 = mybir.dt.float32
F32R = mybir.dt.float32r
BF16 = mybir.dt.bfloat16
I32 = mybir.dt.int32
ALU = mybir.AluOpType
ACT = mybir.ActivationFunctionType
AX = mybir.AxisListType.X

P = 128
D = 1024
KD = D // P
S = 256
TT = S // P
L = 2
CHUNK = 64
WIDTH = 512
KW = WIDTH // P
NE = 64
PAIRS = NE // 2
FE = 256
KF = FE // P
SLOTS = 64
ROUNDS = S // SLOTS
GROUPS = 8
TOPK_GROUPS = 4
ROUTED_SCALE = 2.5
ALPHA = (2 * L) ** 0.25
LN_EPS = 1e-5
RMS_EPS = 1e-5
REL_CLIP = 256
NEG = -1e30
POOL_WINDOWS = (2, 4, 8, 16)
ROPE_THETA = 500000.0
ROPE_DIM = 16

CONST = {}
CONST_COLS = 0
for _name, _width in (("ident", P), ("cos", S), ("sin", S), ("rotate", P), ("mask", S), ("iota", SLOTS),
                      ("earlier", GROUPS * GROUPS), ("ones", P), ("ramp", 4 * 16), ("before", P)):
    CONST[_name] = (CONST_COLS, CONST_COLS + _width)
    CONST_COLS += _width

Z_BLOCKS = [("qa", 0), ("ka", 512), ("va", 1024), ("qc", 2048), ("kc", 2560), ("vc", 3072), ("ub", 1536),
            ("ga", 3584), ("ga", 4096), ("gb", 4608), ("gb", 5120), ("gc", 5632), ("gc", 6144)]
BLOCKS = ([("z", b) for b in range(9)] + [("branch", 0)] + [("z", 9), ("z", 10), ("branch", 1)]
          + [("z", 11), ("z", 12), ("branch", 2), ("out", 0), ("out", 1), ("shared_up", 0), ("shared_down", 0)])
NB = len(BLOCKS)
WBUFS = 3
UNITS = 8


def unit(i):
    return i // 4, (i % 4) // 2, i % 2


def plan():
    sc = lambda i: [("scores", i, 0), ("scores", i, 1)]
    tr = lambda i: [("turn", i, j) for j in range(2 if unit(i)[0] == 0 else 1)]
    after = {
        4: sc(0), 5: sc(1), 6: tr(0) + sc(2), 7: [("pv", 0, 0)] + tr(1) + sc(3),
        8: [("pv", 1, 0)] + tr(2) + [("rope", 0, 0), ("rope", 0, 1)], 9: [("pv", 2, 0)] + tr(3),
        10: [("pv", 3, 0), ("rope", 1, 0), ("rope", 1, 1)], 11: sc(4), 12: sc(5), 13: tr(4) + sc(6),
        14: [("pv", 4, 0)] + tr(5) + sc(7), 15: [("pv", 5, 0)] + tr(6), 16: [("pv", 6, 0)] + tr(7),
        17: [("pv", 7, 0)] + [("branch", 0, j) for j in range(4)], 18: [("pool", 0, 0), ("pool", 1, 0)],
        19: [("rms", 0, 0), ("rms", 1, 0)],
        21: [("branch", 1, j) for j in range(4)], 25: [("branch", 2, j) for j in range(4)],
    }
    tasks = [("xt", 0, g) for g in range(4)]
    for u in range(2 * len(Z_BLOCKS)):
        tasks.append(("z", u, 0))
        tasks += after.get(u, [])
    return tasks + [("xt", 1, g) for g in range(4)] + [("router", 0, 0), ("shared", 0, 0), ("shared", 1, 0),
                                                       ("rank", 0, 0)]


PLAN = plan()
NT = len(PLAN)
INDEX = {task: n for n, task in enumerate(PLAN)}
RING = 4
CHUNKS = []
for _kind, _b in BLOCKS:
    if _kind in ("z", "branch"):
        CHUNKS += [(_kind, _b, 0), (_kind, _b, 1)]
NC = len(CHUNKS)
CHUNK_AT = {c: n for n, c in enumerate(CHUNKS)}
LAST_TASK = [("z", 2 * b + h, 0) if kind == "z" else ("branch", b, 2 * h + 1) for kind, b, h in CHUNKS]
AFTER_TASK = {task: n + WBUFS for n, task in enumerate(LAST_TASK) if n + WBUFS < NC}
BLOCK_OF_Z = {b: n for n, (kind, b) in enumerate(BLOCKS) if kind == "z"}
BLOCK_OF = {(kind, b): n for n, (kind, b) in enumerate(BLOCKS) if kind != "z"}


def build(nc, x, w_in, rel_bias, pool_w, pool_scale, lambda_q1, lambda_k1, lambda_q2, lambda_k2, subln_g,
          w_branch_a, w_branch_b, w_branch_c, w_out, ln1_g, ln1_b, router_w, router_bias,
          expert_w_gate_up, expert_w_down, shared_w_gate_up, shared_w_down, ln2_g, ln2_b, consts, lambda_init,
          out):
    with ExitStack() as ctx:
        def sb(name, shape, dt=F32):
            return ctx.enter_context(nc.sbuf_tensor(name, shape, dt))

        def sem(name):
            return ctx.enter_context(nc.semaphore(name))

        ring_w = sb("ring_w", [P, 2, 4096])
        x_tok = sb("x_tok", [P, TT, D])
        cst = sb("cst", [P, CONST_COLS - P])
        ln_gb = sb("ln_gb", [P, 2, D])
        pool_w_sb = sb("pool_w_sb", [P, KW, P])
        pool_s_sb = sb("pool_s_sb", [P, L, KW])
        subln_sb = sb("subln_sb", [P, L])
        router_sb = sb("router_sb", [P, KD, NE])
        rbias_sb = sb("rbias_sb", [P, L, NE])
        before_b = sb("before_b", [P, P], BF16)
        ones_b = sb("ones_b", [P, P], BF16)
        ident_b = sb("ident_b", [P, P], BF16)
        gate_s = sb("gate_s", [P, 1])
        eps = sb("eps", [P, 2])
        nlam = sb("nlam", [P, L])
        lam_sum = sb("lam_sum", [P, L, 2])
        neg_max = sb("neg_max", [P, 2, 4])
        sums = sb("sums", [P, 2, 4])
        recips = sb("recips", [P, 2, 4])
        stats = sb("stats", [P, 2, 6])
        mean_var = sb("mean_var", [P, TT, 2])
        std = sb("std", [P, TT])
        rstd = sb("rstd", [P, TT])
        sel_b = sb("sel_b", [P, TT, NE], BF16)
        group_s = sb("group_s", [P, TT, GROUPS])
        group_r = sb("group_r", [P, TT, GROUPS])
        wsum = sb("wsum", [P, TT])
        count_f = sb("count_f", [P, 1])
        count_i = sb("count_i", [P, L], I32)
        slot_of = sb("slot_of", [P, TT, ROUNDS * NE + 2])
        gate_of = sb("gate_of", [P, TT, ROUNDS * NE + 2])

        def region(name, size):
            first = (nc.sbuf_base + 31) // 32 * 32
            sb(name, [P, size // 4])
            return lambda n, offset, shape, dt=F32: nc.alloc_sbuf_tensor_at(n, shape, dt, offset=first + offset)

        KB = 1024
        place = region("weights_region", 48 * KB)
        gu_a = place("gu_a", 0, [P, 2, KD, 2 * FE])
        dn_a = place("dn_a", 32 * KB, [P, 2, KF, D])
        w_hi = [place(f"w_hi{n}", 16 * n * KB, [P, KD, S], F32R) for n in range(WBUFS)]
        w_lo = [place(f"w_lo{n}", (16 * n + 8) * KB, [P, KD, S], F32R) for n in range(WBUFS)]
        place = region("x_region", 16 * KB)
        x_hi = place("x_hi", 0, [P, KD, S], F32R)
        x_lo = place("x_lo", 8 * KB, [P, KD, S], F32R)
        x_t = place("x_t", 0, [P, KD, S])
        dn_c = place("dn_c", 0, [P, 2, KF, D])
        score = place("score", 8 * KB, [P, TT, NE])
        choice = place("choice", 8 * KB + 512, [P, TT, NE])
        replaced = place("replaced", 9 * KB, [P, TT, NE])
        sel = place("sel", 9 * KB + 512, [P, TT, NE])
        top = place("top", 10 * KB, [P, TT * GROUPS, 8])
        beats = place("beats", 10 * KB + 512, [P, TT, GROUPS, GROUPS])
        ties = place("ties", 11 * KB, [P, TT, GROUPS, GROUPS])
        sh_silu = place("sh_silu", 12 * KB, [P, KF, S])[:]
        sh_t = place("sh_t", 14 * KB, [P, KF, S])[:]

        arena_at = (nc.sbuf_base + 31) // 32 * 32
        arena = sb("arena", [P, 20480])

        def view(at, *shape, dt=F32):
            size = 1
            for n in shape:
                size *= n
            words = size if dt == F32 else size // 2
            v = arena[:, at:at + words]
            if dt != F32:
                v = v.bitcast(dt)
            if len(shape) == 2:
                v = v.rearrange("p (a b) -> p a b", a=shape[0])
            elif len(shape) == 3:
                v = v.rearrange("p (a b c) -> p a b c", a=shape[0], b=shape[1])
            return v

        gu_b = view(0, 2, KD, 2 * FE)
        dn_b = view(8192, 2, KF, D)
        parts = [view(12288 + 1024 * n, TT, KD, P, dt=BF16) for n in range(3)]
        xe_t = view(15360, KD, P)
        y_hi = nc.alloc_sbuf_tensor_at("y_hi", [P, D], F32R, offset=arena_at + 4 * 16384)
        y_lo = nc.alloc_sbuf_tensor_at("y_lo", [P, D], F32R, offset=arena_at + 4 * 18816)
        onehot_t = nc.alloc_sbuf_tensor_at("onehot_t", [P, S], F32R, offset=arena_at + 4 * 17664)
        gates = view(17408, TT, P)
        silu_g = view(17920, FE)
        hid = view(18176, FE)
        hid_t = view(18432, KF, P)
        onehot = view(18688, TT, P, dt=BF16)
        gu = [gu_a[:], gu_b, ring_w[:].rearrange("p e (k n) -> p e k n", k=KD)]
        dn = [dn_a[:], dn_b, dn_c[:]]
        rest = [xe_t, view(16384, KD, P)]

        qa_t, ka_t, va = view(0, KW, S), view(1024, KW, S), view(2048, TT, WIDTH)
        qc_t, kc_t, vc = view(3072, KW, S), view(4096, KW, S), view(5120, TT, WIDTH)
        ub_t = view(6144, KW, S)
        probs = [view(7168, 4, S), view(8192, 4, S)]
        probs_t = view(9216, 4, 2, P)
        yc_t, mixed, pooled = view(11264, KW, S), view(12288, KW, S), view(13312, KW, S)
        bias_rev = view(14336, 8, S)
        yb_t = view(2048, KW, S)
        sig = view(0, KD, S)
        merged = view(18432, KD, S)
        squares, rms = view(7168, KW, S), view(8192, KW, S)
        lam_in = view(12288, L, 4, CHUNK)
        before_in = view(18432, 1, P)[:, 0, :]
        q_t, k_t = [qa_t, qc_t], [ka_t, kc_t]
        part_at = [(16384, 17408), (14336, 15360), (16384, 17408)]
        y_hi_of, y_lo_of = [[nc.alloc_sbuf_tensor_at(f"y{n}_{part}", [P, KW, S], F32R, offset=arena_at + 4 * at[i])
                             for n, at in zip("abc", part_at)] for i, part in enumerate(("hi", "lo"))]

        banks = [ctx.enter_context(nc.psum_tensor(f"bank{n}", [P, 512], F32)) for n in range(8)]
        acc = [[banks[2 * t + h] for h in range(2)] for t in range(TT)]
        bank_gather, bank_even, bank_odd, bank_t = banks[4:8]

        def const(name):
            a, b = CONST[name]
            return cst[:, a:b]

        ident = const("ident")

        x_in = [sem(f"x_in{t}") for t in range(TT)]
        const_in = sem("const_in")
        first_in = sem("first_in")
        small_in = sem("small_in")
        params_in = sem("params_in")
        bias_in = sem("bias_in")
        ln_in = sem("ln_in")
        block_in = [sem("block_in0"), sem("block_in1")]
        gu_in = [sem(f"gu_in{n}") for n in range(3)]
        dn_in = [sem(f"dn_in{n}") for n in range(3)]
        out_done = sem("out_done")
        bank_ready = sem("bank_ready")
        bank_free = [sem(f"bank_free{n}") for n in range(RING)]
        setup_done = sem("setup_done")
        setup_pool = sem("setup_pool")
        x_hi_ready = sem("x_hi_ready")
        y_hi_ready_of = [sem(f"y{n}_hi_ready") for n in "abc"]
        y_lo_ready_of = [sem(f"y{n}_lo_ready") for n in "abc"]
        w_hi_ready = sem("w_hi_ready")
        w_lo_ready = sem("w_lo_ready")
        lam_ready = sem("lam_ready")
        lam_exp = sem("lam_exp")
        bias_masked = sem("bias_masked")
        max_ready = sem("max_ready")
        exp_ready = sem("exp_ready")
        recip_ready = sem("recip_ready")
        scaled = sem("scaled")
        probs_ready = sem("probs_ready")
        rope_ready = sem("rope_ready")
        mixed_ready = sem("mixed_ready")
        squares_ready = sem("squares_ready")
        yc_ready = sem("yc_ready")
        merged_ready = sem("merged_ready")
        h_ready = sem("h_ready")
        var_ready = sem("var_ready")
        std_ready = sem("std_ready")
        ln_done = sem("ln_done")
        sel_ready = sem("sel_ready")
        count_ready = sem("count_ready")
        part_ready = sem("part_ready")
        rest_ready = sem("rest_ready")
        shared_down = sem("shared_down")
        s_ready = sem("s_ready")
        sg_ready = sem("sg_ready")
        gathered = sem("gathered")
        xe_ready = sem("xe_ready")
        up_done = sem("up_done")
        silu_ready = sem("silu_ready")
        hid_ready = sem("hid_ready")
        hid_turned = sem("hid_turned")
        hid_t_ready = sem("hid_t_ready")
        slots_turned = sem("slots_turned")
        gate_s_ready = sem("gate_s_ready")
        onehot_t_ready = sem("onehot_t_ready")
        y_done = sem("y_done")
        y_hi_ready = sem("y_hi_ready")
        y_ready = sem("y_ready")
        combined = sem("combined")
        acc_done = sem("acc_done")
        dve_step = sem("dve_step")
        loads_cleared = sem("loads_cleared")

        def at(l, task):
            n = l * NT + INDEX[task]
            return n, n % RING, n // RING

        def bank(l, task):
            return banks[4 + at(l, task)[1]]

        def wait_task(eng, l, task):
            eng.wait_ge(bank_ready, at(l, task)[0] + 1)

        def wait_evac(eng, l, task):
            _, b, uses = at(l, task)
            eng.wait_ge(bank_free[b], uses + 1)

        def free(ins, l, task):
            ins.then_inc(bank_free[at(l, task)[1]], 1)

        def more_rounds(eng, l):
            eng.wait_ge(count_ready, l + 1)
            most = eng.value_load(count_i[0:1, l:l + 1], min_val=0, max_val=S - 1)
            return eng.snap(most >> 6).with_bounds(min_val=0, max_val=ROUNDS - 1)

        def x_tile(t, j):
            return t[:, 4 * (j % 2):4 * (j % 2) + 4, P * (j // 2):P * (j // 2) + P]

        def chunk_in(n):
            kind, b, h = CHUNKS[n]
            if kind == "z":
                return ring_w[:, BLOCK_OF_Z[b] % 2, :].rearrange("p (k n) -> p k n", k=KD)[:, :, S * h:S * h + S]
            return ring_w[:, BLOCK_OF[kind, b] % 2, :].rearrange("p (k n) -> p k n", k=KW)[:, :, WIDTH * h:WIDTH * h + WIDTH]

        def chunk_part(buffers, n):
            part = buffers[n % WBUFS][:]
            return part if CHUNKS[n][0] == "z" else part.rearrange("p (k a) n -> p k (a n)", k=KW)

        HALVES = PAIRS // 2
        SIX, LONG = 6, 4
        SHORT_FROM = 2 + SIX * LONG
        IN_LONG = SHORT_FROM // 3 + 1
        assert SHORT_FROM % 3 == 2 and SHORT_FROM % 2 == 0 and SHORT_FROM < PAIRS

        def short_steps(more):
            return more * HALVES + (HALVES - SHORT_FROM // 2)

        def loads_before(l, shorts, slot):
            return l * (IN_LONG - 1) if slot == 2 else l * IN_LONG + shorts

        def norm_std(act, l, which, t):
            act.wait_ge(var_ready, TT * (2 * l + which) + t + 1)
            nc.scalar.activation(std[:, t:t + 1], mean_var[:, t, 1:2], ACT.Sqrt,
                                 bias=eps[:, 0:1]).then_inc(std_ready, 1)

        block = ctx.enter_context(nc.Block())

        @block.sync
        def _(sp):
            sp.dma_start(cst[:, 0:P], consts[:, 0:P]).then_inc(x_in[0], 16)
            for t in range(TT):
                sp.dma_start(x_tok[:, t, :], x[0, P * t:P * t + P, :]).then_inc(x_in[t], 16)

            def load_block(l, n):
                kind, b = BLOCKS[n]
                slot, before = n % 2, n - 2
                bl = l if before >= 0 else l - 1
                before %= NB
                if bl >= 0:
                    if BLOCKS[before][0] in ("z", "branch"):
                        sp.wait_ge(w_lo_ready, NC * bl + CHUNK_AT[*BLOCKS[before], 1] + 1)
                    elif BLOCKS[before][0] == "shared_up":
                        wait_task(sp, bl, ("shared", 1, 0))
                    elif BLOCKS[before][0] == "out":
                        sp.wait_ge(h_ready, 2 * TT * (bl + 1))
                    else:
                        sp.wait_ge(shared_down, bl + 1)
                if kind == "z":
                    c = Z_BLOCKS[b][1]
                    dst = ring_w[:, slot, :].rearrange("p (k n) -> p k n", k=KD)
                    src = w_in[l, :, c:c + WIDTH].rearrange("(p k) n -> p k n", k=KD)
                    if (l, n) == (0, 0):
                        sp.dma_start(dst[:, :, 0:S], src[:, :, 0:S]).then_inc(first_in, 16)
                        sp.dma_start(cst[:, P:], consts[:, P:CONST["before"][0]]).then_inc(const_in, 16)
                        sp.dma_start(before_in, consts[:, CONST["before"][0]:]).then_inc(const_in, 16)
                        dst, src = dst[:, :, S:], src[:, :, S:]
                elif kind == "branch":
                    dst = ring_w[:, slot, :].rearrange("p (k n) -> p k n", k=KW)
                    src = (w_branch_a, w_branch_b, w_branch_c)[b][l].rearrange("(k p) n -> p k n", p=P)
                elif kind == "out":
                    dst = ring_w[:, slot, :].rearrange("p (k n) -> p k n", k=KD)
                    src = w_out[l, :, 512 * b:512 * b + 512].rearrange("(k p) n -> p k n", p=P)
                elif kind == "shared_up":
                    dst = ring_w[:, slot, :]
                    src = shared_w_gate_up[l].rearrange("(p k) n -> p (k n)", k=KD)
                else:
                    dst = ring_w[:, slot, 0:KF * D].rearrange("p (k n) -> p k n", k=KF)
                    src = shared_w_down[l].rearrange("(k p) n -> p k n", p=P)
                sp.dma_start(dst, src).then_inc(block_in[slot], 16)

            def load_up(l, slot, pair, experts=(0, 2)):
                if slot == 2 and experts == (0, 2):
                    for e in range(2):
                        load_up(l, slot, pair, (e, e + 1))
                    return
                a, b = experts
                sp.dma_start(gu[slot][:, a:b], expert_w_gate_up[l, bass.ds(2 * pair + a, b - a)]
                             .rearrange("e (p k) n -> p e k n", k=KD)).then_inc(gu_in[slot], 16)

            def load_down(l, slot, pair):
                sp.dma_start(dn[slot], expert_w_down[l, bass.ds(2 * pair, 2)]
                             .rearrange("e (p k) n -> p e k n", k=KF)).then_inc(dn_in[slot], 16)

            def load_after(l, slot, pair, used):
                sp.wait_ge(up_done, used)
                sp.sem_inc(loads_cleared, 1)
                load_up(l, slot, pair)
                sp.wait_ge(y_done, 2 * used)
                sp.sem_inc(loads_cleared, 1)
                load_down(l, slot, pair)

            start = 0
            for l in range(L):
                for n in range(NB - 2):
                    load_block(l, n)
                wait_task(sp, l, ("branch", 2, 3))
                load_up(l, 0, 0)
                load_down(l, 0, 0)
                sp.wait_ge(merged_ready, 4 * (l + 1))
                load_up(l, 1, 1)
                sp.wait_ge(h_ready, 2 * TT * (l + 1))
                for n in range(NB - 2, NB):
                    load_block(l, n)
                load_down(l, 1, 1)
                wait_task(sp, l, ("shared", 1, 0))
                load_up(l, 2, 2, (0, 1))
                sp.wait_ge(shared_down, l + 1)
                load_up(l, 2, 2, (1, 2))
                more = more_rounds(sp, l)
                load_down(l, 2, 2)
                with sp.Fori(0, SHORT_FROM // 3 - 1) as i:
                    for u in range(3):
                        load_after(l, u, 3 * i + 3 + u, 2 * start + 3 * i + u + 1)
                for n in range(SHORT_FROM - 2, SHORT_FROM):
                    load_after(l, n % 3, n, 2 * start + n - 2)
                with sp.Fori(0, short_steps(more)) as i:
                    pair = 2 * ((i + SHORT_FROM // 2) & (HALVES - 1))
                    for u in range(2):
                        load_after(l, u, pair + u, 2 * (i + start) + SHORT_FROM + u - 1)
                start = start + more * HALVES + HALVES
            for t in range(TT):
                sp.wait_ge(ln_done, TT * (2 * L - 1) + t + 1)
                sp.dma_start(out[0, P * t:P * t + P, :], x_tok[:, t, :]).then_inc(out_done, 16)
            sp.wait_ge(out_done, 16 * TT)

        @block.gpsimd
        def _(pool):
            pool.memset(slot_of[:, :, ROUNDS * NE:], -1.0).then_inc(setup_pool, 1)
            pool.memset(gate_of[:, :, ROUNDS * NE:], 0.0).then_inc(setup_pool, 1)

            def split_low(l, n):
                pool.wait_ge(w_hi_ready, NC * l + n + 1)
                pool.tensor_tensor(chunk_part(w_lo, n), chunk_in(n), chunk_part(w_hi, n).bitcast(F32),
                                   ALU.subtract).then_inc(w_lo_ready, 1)

            for l in range(L):
                for u in range(WBUFS):
                    split_low(l, u)
                pool.wait_ge(bias_in, 16 * (l + 1))
                pool.memset(bias_rev[0:CHUNK, :, 0:CHUNK], NEG).then_inc(bias_masked, 1)
                for task in PLAN:
                    kind, i, j = task
                    if task in AFTER_TASK:
                        split_low(l, AFTER_TASK[task])
                    if kind != "scores" or j == 0:
                        continue
                    g = l * UNITS + i
                    branch, qt, _ = unit(i)
                    W = P * (qt + 1)
                    p = probs[i % 2][:, :, 0:W]
                    pool.wait_ge(recip_ready, g + 1)
                    scale = recips[:, i % 2, :].unsqueeze(2).to_broadcast([P, 4, W])
                    ins = pool.tensor_tensor(p, p, scale, ALU.mult)
                    if branch == 0:
                        ins.then_inc(probs_ready, 1)
                    else:
                        ins.then_inc(scaled, 1)
                        pool.wait_ge(scaled, l * 4 + i - 3)
                        pool.tensor_tensor(p[:, 0::2, :], p[:, 0::2, :], p[:, 1::2, :], ALU.add).then_inc(probs_ready, 1)
                for t in range(TT):
                    for n in range(2):
                        k = 3 * TT * l + 3 * t + n
                        pool.wait_ge(part_ready, k + 1)
                        src = x_tok[:, t, :].rearrange("p (q k) -> p k q", k=KD) if n == 0 else rest[t]
                        if n:
                            pool.wait_ge(rest_ready, 2 * TT * l + 2 * t + n)
                        pool.tensor_tensor(rest[t], src, parts[n][:, t], ALU.subtract).then_inc(rest_ready, 1)

        @block.scalar
        def _(act):
            def load_ln(l, which):
                g, b = ((ln1_g, ln1_b), (ln2_g, ln2_b))[which]
                act.dma_start(ln_gb[:, 0, :], g[l].partition_broadcast(P)).then_inc(ln_in, 16)
                act.dma_start(ln_gb[:, 1, :], b[l].partition_broadcast(P)).then_inc(ln_in, 16)

            def load_bias(l):
                head = 2 * REL_CLIP + 1
                rows = bass.AP(tensor=rel_bias.tensor, offset=rel_bias.offset + l * 8 * head + REL_CLIP - P + 1,
                               ap=[[1, P], [head, 8], [1, S]])
                act.dma_start(bias_rev, rows).then_inc(bias_in, 16)

            def load_params(l):
                act.dma_start(router_sb[:], router_w[l].rearrange("(p k) e -> p k e", k=KD)).then_inc(params_in, 16)
                act.dma_start(pool_w_sb[:], pool_w[l].rearrange("g c d -> c g d")).then_inc(params_in, 16)

            def load_smalls():
                for l in range(L):
                    for n, vec in enumerate((lambda_q1, lambda_k1, lambda_q2, lambda_k2)):
                        act.dma_start(lam_in[:, l, n, :], vec[l].partition_broadcast(P)).then_inc(small_in, 16)
                    act.dma_start(rbias_sb[:, l, :], router_bias[l].partition_broadcast(P)).then_inc(small_in, 16)
                    with nc.allow_non_contiguous_dma(reason="a few hundred words, once"):
                        act.dma_start(pool_s_sb[:, l], pool_scale[l].rearrange("(g p) -> p g", p=P)).then_inc(small_in, 16)
                        act.dma_start(subln_sb[:, l:l + 1], subln_g[l].rearrange("(p a) -> p a", a=1)).then_inc(small_in, 16)

            def split_high(l, n):
                kind, b, h = CHUNKS[n]
                block = BLOCK_OF_Z[b] if kind == "z" else BLOCK_OF[kind, b]
                if (l, n) == (0, 0):
                    act.wait_ge(first_in, 16)
                elif h == 0 or (l, n) == (0, 1):
                    act.wait_ge(block_in[block % 2], 16 * (l * (NB // 2) + block // 2 + 1))
                nc.scalar.copy(chunk_part(w_hi, n), chunk_in(n)).then_inc(w_hi_ready, 1)

            start = 0
            for l in range(L):
                for task in PLAN:
                    kind, i, j = task
                    b = bank(l, task)
                    if l == 0 and task == ("z", 2, 0):
                        act.wait_ge(lam_ready, 1)
                        nc.scalar.activation(lam_sum[:], lam_sum[:], ACT.Exp).then_inc(lam_exp, 1)
                    if kind == "xt" and i == 0:
                        wait_task(act, l, task)
                        nc.scalar.copy(x_tile(x_hi, j), b[:].rearrange("p (c n) -> p c n", c=4)).then_inc(x_hi_ready, 1)
                        if j == 3:
                            if l == 0:
                                for u in range(WBUFS):
                                    split_high(0, u)
                                    if u == 0:
                                        load_smalls()
                                        load_bias(0)
                                        load_params(0)
                            else:
                                act.wait_ge(ln_done, TT * 2 * l)
                            load_ln(l, 0)
                    elif kind == "xt" and j % 2 == 0:
                        wait_task(act, l, task)
                        free(nc.scalar.copy(x_tile(x_t, j), b[:].rearrange("p (c n) -> p c n", c=4)), l, task)
                    elif kind == "z":
                        wait_task(act, l, task)
                        name, half = Z_BLOCKS[i // 2][0], i % 2
                        two = b[:].rearrange("p (c n) -> p c n", c=2)
                        if name in ("ga", "gb", "gc"):
                            v = (i - 14) % 4
                            if name != "ga":
                                wait_evac(act, l, ("branch", 0 if name == "gb" else 1, v))
                            ins = nc.scalar.activation(sig[:, 2 * v:2 * v + 2, :], two, ACT.Sigmoid)
                        elif name in ("va", "vc"):
                            ins = nc.scalar.copy((va if name == "va" else vc)[:, :, S * half:S * half + S], two)
                        else:
                            dst = {"qa": qa_t, "ka": ka_t, "qc": qc_t, "kc": kc_t, "ub": ub_t}[name]
                            ins = nc.scalar.copy(dst[:, 2 * half:2 * half + 2, :], two)
                        free(ins, l, task)
                    elif kind == "scores" and j == 1:
                        g, W = l * UNITS + i, P * (unit(i)[1] + 1)
                        act.wait_ge(max_ready, g + 1)
                        for m in range(4):
                            p = probs[i % 2][:, m, 0:W]
                            ins = nc.scalar.activation(p, p, ACT.Exp, bias=neg_max[:, i % 2, m:m + 1],
                                                       accum_out=sums[:, i % 2, m:m + 1])
                        ins.then_inc(exp_ready, 1)
                    elif kind == "turn":
                        wait_task(act, l, task)
                        branch, qt, _ = unit(i)
                        s0 = 2 * j if branch == 0 else 0
                        free(nc.scalar.copy(probs_t[:, s0:s0 + 2, 0:qt + 1, :],
                                            b[:, 0:2 * (qt + 1) * P].rearrange("p (m k n) -> p m k n", m=2, k=qt + 1)),
                             l, task)
                    elif kind == "rms":
                        wait_task(act, l, task)
                        free(nc.scalar.activation(rms[:, 2 * i:2 * i + 2, :], b[:].rearrange("p (c n) -> p c n", c=2),
                                                  ACT.Sqrt, bias=eps[:, 1:2], scale=1.0 / P), l, task)
                    elif kind == "router":
                        wait_task(act, l, task)
                        free(nc.scalar.activation(score[:], b[:, 0:TT * NE].rearrange("p (t e) -> p t e", t=TT),
                                                  ACT.Exp, scale=-1.0), l, task)
                    elif kind == "shared" and i == 0:
                        wait_task(act, l, task)
                        free(nc.scalar.activation(sh_silu, b[:].rearrange("p (c n) -> p c n", c=2), ACT.Silu), l, task)
                    elif kind == "pv" and unit(i)[0] == 0:
                        wait_task(act, l, task)
                        _, qt, g = unit(i)
                        nc.scalar.copy(y_hi_of[0][:, 2 * g:2 * g + 2, P * qt:P * qt + P],
                                       b[:, 0:2 * P].rearrange("p (c n) -> p c n", c=2)).then_inc(y_hi_ready_of[0], 1)
                    if task in (("pool", 1, 0), ("z", 21, 0)):
                        n = 1 if kind == "pool" else 2
                        if n == 1:
                            wait_evac(act, l, ("pool", 0, 0))
                            wait_evac(act, l, ("pool", 1, 0))
                        else:
                            act.wait_ge(yc_ready, 2 * (l + 1))
                            wait_task(act, l, ("branch", 0, 3))
                        nc.scalar.copy(y_hi_of[n][:], (yb_t, yc_t)[n - 1]).then_inc(y_hi_ready_of[n], 1)
                    if task in AFTER_TASK:
                        if kind == "branch":
                            wait_task(act, l, task)
                        split_high(l, AFTER_TASK[task])
                    if task == ("branch", 2, 3):
                        for t in range(TT):
                            norm_std(act, l, 0, t)
                    if task == ("xt", 1, 2):
                        act.wait_ge(ln_done, TT * 2 * l + TT)
                        load_ln(l, 1)

                if l + 1 < L:
                    load_params(l + 1)

                for t in range(TT):
                    for n in range(3):
                        src = x_tok[:, t, :].rearrange("p (q k) -> p k q", k=KD) if n == 0 else rest[t]
                        if n:
                            act.wait_ge(rest_ready, 2 * TT * l + 2 * t + n)
                        nc.scalar.copy(parts[n][:, t], src).then_inc(part_ready, 1)

                def gather_out(n, half):
                    act.wait_ge(gathered, 2 * (n + l) + half + 1)
                    nc.scalar.copy(xe_t[:, 4 * half:4 * half + 4, :],
                                   bank_gather[:].rearrange("p (c n) -> p c n", c=4)).then_inc(xe_ready, 1)

                def pair_step(n, odd):
                    bank_up, bank_other = (bank_even, bank_odd)[::-1 if odd else 1]
                    act.wait_ge(up_done, n + 1)
                    nc.scalar.activation(silu_g, bank_up[:, 0:FE], ACT.Silu).then_inc(silu_ready, 1)
                    for h in range(2):
                        act.wait_ge(y_done, 2 * n + h + 1)
                        nc.scalar.copy(y_hi[:, 512 * h:512 * h + 512], (bank_other, bank_up)[h][:]).then_inc(y_hi_ready, 1)
                        gather_out(n + 1, h)

                more = more_rounds(act, l)
                gather_out(2 * start, 0)
                gather_out(2 * start, 1)
                for n in range(2):
                    pair_step(2 * start + n, n)
                with act.Fori(0, LONG) as i:
                    for u in range(SIX):
                        pair_step(2 * start + SIX * i + 2 + u, u % 2)
                with act.Fori(0, short_steps(more)) as i:
                    for u in range(2):
                        pair_step(2 * (i + start) + SHORT_FROM + u, u)
                start = start + more * HALVES + HALVES
                if l + 1 < L:
                    act.wait_ge(y_done, 4 * start)
                    split_high(l + 1, 0)
                for t in range(TT):
                    norm_std(act, l, 1, t)
                    if l + 1 < L:
                        split_high(l + 1, t + 1)
                if l + 1 < L:
                    act.wait_ge(xe_ready, 2 * (2 * start + l) + 2)
                    act.sem_inc(loads_cleared, 1)
                    load_bias(l + 1)

        @block.vector
        def _(dve):
            steps = [0]

            def step(ins):
                ins.then_inc(dve_step, 1)
                steps[0] += 1

            def settle():
                dve.wait_ge(dve_step, steps[0])

            v = nc.vector
            dve.wait_ge(x_in[0], 32)
            dve.wait_ge(const_in, 32)
            v.tensor_copy(before_b[:], before_in).then_inc(setup_done, 1)
            v.tensor_copy(ones_b[:], const("ones")).then_inc(setup_done, 1)
            v.tensor_copy(ident_b[:], ident).then_inc(setup_done, 1)
            v.memset(eps[:, 0:1], LN_EPS).then_inc(setup_done, 1)
            v.memset(eps[:, 1:2], RMS_EPS).then_inc(setup_done, 1)
            dve.wait_ge(setup_done, 5)
            def lambdas():
                dve.wait_ge(small_in, 16 * 7 * L)
                for l in range(L):
                    step(v.tensor_tensor(lam_in[:, l, 0::2, :], lam_in[:, l, 0::2, :], lam_in[:, l, 1::2, :], ALU.mult))
                    step(v.tensor_scalar(subln_sb[:, l:l + 1], subln_sb[:, l:l + 1], 1.0 - lambda_init[l], None, ALU.mult))
                settle()
                for l in range(L):
                    ins = v.tensor_reduce(lam_sum[:, l, :], lam_in[:, l, 0::2, :], AX, ALU.add)
                    if l < L - 1:
                        step(ins)
                ins.then_inc(lam_ready, 1)
                dve.wait_ge(lam_exp, 1)
                step(v.tensor_tensor(nlam[:], lam_sum[:, :, 1], lam_sum[:, :, 0], ALU.subtract))
                settle()
                for l in range(L):
                    step(v.tensor_scalar(nlam[:, l:l + 1], nlam[:, l:l + 1], -lambda_init[l], None, ALU.add))

            def norm(l, which):
                k = 2 * l + which
                dve.wait_ge(ln_in, 32 * (k + 1))
                for t in range(TT):
                    row = x_tok[:, t, :]
                    for h in range(2):
                        if which == 0:
                            dve.wait_ge(h_ready, 2 * TT * l + 2 * t + h + 1)
                        else:
                            dve.wait_ge(acc_done, 2 * TT * l + TT * h + t + 1)
                        part = x_tok[:, t, 512 * h:512 * h + 512]
                        step(v.scalar_tensor_tensor(out=part, in0=part, scalar=ALPHA, in1=acc[t][h][:],
                                                    op0=ALU.mult, op1=ALU.add))
                        settle()
                        step(v.bn_stats(stats[:, h, :], part))
                    settle()
                    v.bn_aggr(mean_var[:, t, :], stats[:].rearrange("p a b -> p (a b)")).then_inc(var_ready, 1)
                    dve.wait_ge(var_ready, TT * k + t + 1)
                    step(v.scalar_tensor_tensor(out=row, in0=row, scalar=mean_var[:, t, 0:1], in1=ln_gb[:, 0, :],
                                                op0=ALU.subtract, op1=ALU.mult))
                    dve.wait_ge(std_ready, TT * k + t + 1)
                    step(v.reciprocal(rstd[:, t:t + 1], std[:, t:t + 1]))
                    settle()
                    v.scalar_tensor_tensor(out=row, in0=row, scalar=rstd[:, t:t + 1], in1=ln_gb[:, 1, :],
                                           op0=ALU.mult, op1=ALU.add).then_inc(ln_done, 1)

            def pool_windows(l):
                wait_evac(dve, l, ("z", 12, 0))
                wait_evac(dve, l, ("z", 13, 0))
                dve.wait_ge(rope_ready, 4 * (l + 1))
                src, dst, other = ub_t, mixed, pooled
                for level in range(4):
                    n = 1 << level
                    g = slice(level, KW)
                    step(v.tensor_tensor(dst[:, g, n:], src[:, g, n:], src[:, g, :S - n], ALU.add))
                    step(v.tensor_copy(dst[:, g, 0:n], src[:, g, 0:n]))
                    settle()
                    src, dst, other = dst, other, dst
                for g, w in enumerate(POOL_WINDOWS):
                    s = (mixed, pooled)[g % 2]
                    ramp = const("ramp")[:, 16 * g:16 * g + 16]
                    step(v.tensor_tensor(s[:, g, 0:16], s[:, g, 0:16], ramp, ALU.mult))
                settle()
                for g, w in enumerate(POOL_WINDOWS):
                    s = (mixed, pooled)[g % 2]
                    ins = v.scalar_tensor_tensor(out=mixed[:, g, :], in0=s[:, g, :], scalar=1.0 / w, in1=ub_t[:, g, :],
                                                 op0=ALU.mult, op1=ALU.subtract)
                    if g < KW - 1:
                        step(ins)
                ins.then_inc(mixed_ready, 1)

            def route(l):
                wait_evac(dve, l, ("router", 0, 0))
                step(v.tensor_scalar(score[:], score[:], 1.0, None, ALU.add))
                settle()
                step(v.reciprocal(score[:], score[:]))
                settle()
                step(v.tensor_tensor(choice[:], score[:], rbias_sb[:, l, :].unsqueeze(1).to_broadcast([P, TT, NE]),
                                     ALU.add))
                settle()
                for t in range(TT):
                    for g in range(GROUPS):
                        step(v.max(top[:, t * GROUPS + g, :], choice[:, t, 8 * g:8 * g + 8]))
                settle()
                step(v.tensor_tensor(group_s[:].rearrange("p t g -> p (t g)"), top[:, :, 0], top[:, :, 1], ALU.add))
                settle()
                one = group_s[:].unsqueeze(3).to_broadcast([P, TT, GROUPS, GROUPS])
                other = group_s[:].unsqueeze(2).to_broadcast([P, TT, GROUPS, GROUPS])
                earlier = const("earlier").unsqueeze(1).to_broadcast([P, TT, GROUPS * GROUPS])
                step(v.tensor_tensor(beats[:], other, one, ALU.is_gt))
                step(v.tensor_tensor(ties[:], other, one, ALU.is_equal))
                settle()
                flat = ties[:].rearrange("p t a b -> p t (a b)")
                step(v.tensor_tensor(flat, flat, earlier, ALU.mult))
                settle()
                step(v.tensor_tensor(beats[:], beats[:], ties[:], ALU.add))
                settle()
                step(v.tensor_reduce(group_r[:], beats[:], AX, ALU.add))
                settle()
                step(v.tensor_scalar(group_r[:], group_r[:], TOPK_GROUPS - 0.5, NEG, ALU.is_gt, ALU.mult))
                settle()
                by_group = choice[:].rearrange("p t (g e) -> p (t g) e", g=GROUPS)
                out_of = group_r[:].rearrange("p t g -> p (t g)").unsqueeze(2).to_broadcast([P, TT * GROUPS, 8])
                step(v.tensor_tensor(by_group, by_group, out_of, ALU.add))
                settle()
                for t in range(TT):
                    step(v.max(top[:, t, :], choice[:, t, :]))
                settle()
                for t in range(TT):
                    step(v.match_replace(out=replaced[:, t, :], in_to_replace=top[:, t, :], in_values=choice[:, t, :],
                                         imm_value=3 * NEG))
                settle()
                v.tensor_tensor(sel_b[:], replaced[:], choice[:], ALU.not_equal).then_inc(sel_ready, 1)
                step(v.tensor_tensor(sel[:], replaced[:], choice[:], ALU.not_equal))
                settle()
                step(v.tensor_tensor(score[:], score[:], sel[:], ALU.mult))
                settle()
                step(v.tensor_reduce(wsum[:], score[:], AX, ALU.add))
                settle()
                step(v.reciprocal(wsum[:], wsum[:]))
                settle()
                for t in range(TT):
                    step(v.tensor_scalar(gate_of[:, t, 0:NE], score[:, t, :], wsum[:, t:t + 1], ROUTED_SCALE,
                                         ALU.mult, ALU.mult))
                settle()
                for r in range(1, ROUNDS):
                    step(v.tensor_copy(gate_of[:, :, r * NE:(r + 1) * NE], gate_of[:, :, 0:NE]))
                step(v.tensor_scalar(choice[:], sel[:], 1000.0, -1000.0, ALU.mult, ALU.add))
                settle()

            def ranks(l):
                task = ("rank", 0, 0)
                b = bank(l, task)
                wait_task(dve, l, task)
                step(v.tensor_tensor(slot_of[:, :, 0:NE], b[:, 0:TT * NE].rearrange("p (t e) -> p t e", t=TT), sel[:],
                                     ALU.mult))
                free(v.tensor_reduce(count_f[:], b[:, TT * NE:(TT + 1) * NE], AX, ALU.max), l, task)
                settle()
                step(v.tensor_tensor(slot_of[:, :, 0:NE], slot_of[:, :, 0:NE], choice[:], ALU.add))
                settle()
                wait_evac(dve, l, task)
                v.tensor_scalar(count_i[:, l:l + 1], count_f[:], -1.0, None, ALU.add).then_inc(count_ready, 1)
                for r in range(1, ROUNDS):
                    step(v.tensor_scalar(slot_of[:, :, r * NE:(r + 1) * NE], slot_of[:, :, 0:NE], float(-SLOTS * r), None,
                                         ALU.add))
                settle()

            def slots(n, l, col):
                iota = const("iota").unsqueeze(1).unsqueeze(1).to_broadcast([P, TT, 2, SLOTS])
                rank = slot_of[:, :, bass.ds(col, 2)].unsqueeze(3).to_broadcast([P, TT, 2, SLOTS])
                gate = gate_of[:, :, bass.ds(col, 2)].unsqueeze(3).to_broadcast([P, TT, 2, SLOTS])
                hot = onehot.rearrange("p t (e c) -> p t e c", e=2)
                if not isinstance(n, int) or n + l:
                    dve.wait_ge(sg_ready, n + l)
                v.tensor_tensor(hot, rank, iota, ALU.is_equal).then_inc(s_ready, 1)
                dve.wait_ge(s_ready, n + l + 1)
                v.tensor_tensor(gates.rearrange("p t (e c) -> p t e c", e=2), hot, gate, ALU.mult).then_inc(sg_ready, 1)

            start = 0
            for l in range(L):
                for task in PLAN:
                    kind, i, j = task
                    b = bank(l, task)
                    pair = b[:].rearrange("p (c n) -> p c n", c=2)
                    if kind == "xt" and i == 0:
                        dve.wait_ge(x_hi_ready, 4 * l + j + 1)
                        free(v.tensor_tensor(x_tile(x_lo, j), b[:].rearrange("p (c n) -> p c n", c=4),
                                             x_tile(x_hi, j).bitcast(F32), ALU.subtract), l, task)
                        if (l, j) == (0, 3):
                            lambdas()
                    elif kind == "xt" and j % 2 == 1:
                        wait_task(dve, l, task)
                        free(v.tensor_copy(x_tile(x_t, j), b[:].rearrange("p (c n) -> p c n", c=4)), l, task)
                    elif kind == "scores":
                        branch, qt, g = unit(i)
                        W = P * (qt + 1)
                        wait_task(dve, l, task)
                        if i >= 2:
                            wait_task(dve, l, ("turn", i - 2, 1 if unit(i - 2)[0] == 0 else 0))
                        if branch == 0:
                            if (i, j) == (0, 0):
                                dve.wait_ge(bias_masked, l + 1)
                            m = 4 * g + j
                            add = bias_rev[:, m:m + 3:2, 0:W][:, :, ::-1]
                        else:
                            add = const("mask")[:, S - W:S].unsqueeze(1).to_broadcast([P, 2, W])
                        free(v.scalar_tensor_tensor(out=probs[i % 2][:, j::2, 0:W],
                                                    in0=b[:, 0:2 * W].rearrange("p (m n) -> p m n", m=2),
                                                    scalar=float(CHUNK) ** -0.5, in1=add, op0=ALU.mult, op1=ALU.add),
                             l, task)
                        if j == 1:
                            wait_evac(dve, l, ("scores", i, 0))
                            wait_evac(dve, l, task)
                            v.tensor_reduce(neg_max[:, i % 2, :], probs[i % 2][:, :, 0:W], AX, ALU.max,
                                            negate=True).then_inc(max_ready, 1)
                            dve.wait_ge(exp_ready, l * UNITS + i + 1)
                            ins = v.reciprocal(recips[:, i % 2, :], sums[:, i % 2, :])
                            if branch == 1:
                                step(ins)
                                settle()
                                odd = recips[:, i % 2, 1::2]
                                ins = v.tensor_scalar(odd, odd, nlam[:, l:l + 1], None, ALU.mult)
                            ins.then_inc(recip_ready, 1)
                    elif kind == "pv":
                        branch, qt, g = unit(i)
                        where = (slice(0, P), slice(2 * g, 2 * g + 2), slice(P * qt, P * qt + P))
                        two = b[:, 0:2 * P].rearrange("p (c n) -> p c n", c=2)
                        if branch == 0:
                            dve.wait_ge(y_hi_ready_of[0], 4 * l + i + 1)
                            ins = v.tensor_tensor(y_lo_of[0][where], two, y_hi_of[0][where].bitcast(F32), ALU.subtract)
                        else:
                            wait_task(dve, l, task)
                            ins = v.tensor_copy(yc_t[where], two)
                        free(ins, l, task)
                        if i == 7:
                            for k in range(4, 8):
                                wait_evac(dve, l, ("pv", k, 0))
                            v.tensor_tensor(squares, yc_t, yc_t, ALU.mult).then_inc(squares_ready, 1)
                    elif kind == "rope":
                        raw = (qc_t, kc_t)[i][:, 2 * j:2 * j + 2, :]
                        wait_task(dve, l, task)
                        if 4 * l + 2 * i + j:
                            dve.wait_ge(rope_ready, 4 * l + 2 * i + j)
                        turned = pooled[:, 0:2, :]
                        plain = pooled[:, 2:4, :]
                        free(v.tensor_tensor(turned, pair, const("sin").unsqueeze(1).to_broadcast([P, 2, S]), ALU.mult),
                             l, task)
                        step(v.tensor_tensor(plain, raw, const("cos").unsqueeze(1).to_broadcast([P, 2, S]), ALU.mult))
                        settle()
                        wait_evac(dve, l, task)
                        v.tensor_tensor(raw, plain, turned, ALU.add).then_inc(rope_ready, 1)
                    elif kind == "pool":
                        wait_task(dve, l, task)
                        for c in range(2):
                            g = 2 * i + c
                            ins = v.tensor_scalar(yb_t[:, g, :], b[:, S * c:S * c + S], pool_s_sb[:, l, g:g + 1], None,
                                                  ALU.mult)
                        free(ins, l, task)
                    elif kind == "rms":
                        wait_evac(dve, l, task)
                        r, y = rms[:, 2 * i:2 * i + 2, :], yc_t[:, 2 * i:2 * i + 2, :]
                        step(v.reciprocal(r, r))
                        settle()
                        v.scalar_tensor_tensor(out=y, in0=y, scalar=subln_sb[:, l:l + 1], in1=r, op0=ALU.mult,
                                               op1=ALU.mult).then_inc(yc_ready, 1)
                    elif kind == "branch":
                        wait_task(dve, l, task)
                        wait_evac(dve, l, ("z", 14 + 4 * i + j, 0))
                        if i:
                            settle()
                        s, m = sig[:, 2 * j:2 * j + 2, :], merged[:, 2 * j:2 * j + 2, :]
                        if i == 0:
                            free(v.tensor_tensor(m, pair, s, ALU.mult), l, task)
                        else:
                            add = pooled[:, 2 * (j % 2):2 * (j % 2) + 2, :]
                            if i == 2 and j >= 2:
                                dve.wait_ge(merged_ready, 4 * l + j - 1)
                            free(v.tensor_tensor(add, pair, s, ALU.mult), l, task)
                            wait_evac(dve, l, task)
                            if i == 1:
                                wait_evac(dve, l, ("branch", 0, j))
                            ins = v.tensor_tensor(m, m, add, ALU.add)
                            if i == 1:
                                step(ins)
                            else:
                                ins.then_inc(merged_ready, 1)
                    elif kind == "shared" and i == 1:
                        wait_task(dve, l, task)
                        wait_evac(dve, l, ("shared", 0, 0))
                        free(v.tensor_tensor(sh_t, sh_silu, pair, ALU.mult), l, task)
                    if task in (("pool", 1, 0), ("z", 21, 0)):
                        n = 1 if kind == "pool" else 2
                        dve.wait_ge(y_hi_ready_of[n], l + 1)
                        v.tensor_tensor(y_lo_of[n][:], (yb_t, yc_t)[n - 1], y_hi_of[n][:].bitcast(F32),
                                        ALU.subtract).then_inc(y_lo_ready_of[n], 1)
                    if task == ("pv", 5, 0):
                        pool_windows(l)
                    if task == ("branch", 2, 3):
                        norm(l, 0)
                    if task == ("router", 0, 0):
                        route(l)
                    if task == ("rank", 0, 0):
                        ranks(l)

                dve.wait_ge(setup_pool, 2)
                slots(2 * start, l, 0)
                more = more_rounds(dve, l)

                def pair_step(n, col, odd, combined_before):
                    bank_up, bank_other = (bank_even, bank_odd)[::-1 if odd else 1]
                    dve.wait_ge(slots_turned, n + 1)
                    v.tensor_copy(gate_s[:], bank_t[:, 0:1]).then_inc(gate_s_ready, 1)
                    slots(n + 1, l, col + 2)
                    dve.wait_ge(gate_s_ready, n + 1)
                    dve.wait_ge(silu_ready, n + 1)
                    v.scalar_tensor_tensor(out=hid, in0=silu_g, scalar=gate_s[:, 0:1], in1=bank_up[:, FE:2 * FE],
                                           op0=ALU.mult, op1=ALU.mult).then_inc(hid_ready, 1)
                    dve.wait_ge(hid_turned, n + 1)
                    v.tensor_copy(hid_t, bank_t[:, 0:FE].rearrange("p (k n) -> p k n", k=KF)).then_inc(hid_t_ready, 1)
                    if combined_before is not None:
                        dve.wait_ge(combined, combined_before)
                    v.tensor_copy(onehot_t[:], bank_t[:, FE:FE + S]).then_inc(onehot_t_ready, 1)
                    for h in range(2):
                        dve.wait_ge(y_hi_ready, 2 * n + h + 1)
                        part = slice(512 * h, 512 * h + 512)
                        v.tensor_tensor(y_lo[:, part], (bank_other, bank_up)[h][:], y_hi[:, part].bitcast(F32),
                                        ALU.subtract).then_inc(y_ready, 1)

                for n in range(2):
                    pair_step(2 * start + n, 2 * n, n, 2 * start - l + 1 if n else None)
                with dve.Fori(0, LONG) as i:
                    for u in range(SIX):
                        n = 2 * start + SIX * i + 2 + u
                        pair_step(n, 2 * SIX * i + 2 * (2 + u), u % 2, n - l)
                with dve.Fori(0, short_steps(more)) as i:
                    for u in range(2):
                        n = 2 * (i + start) + SHORT_FROM + u
                        pair_step(n, 4 * i + 2 * (SHORT_FROM + u), u, n - l)
                start = start + more * HALVES + HALVES
                norm(l, 1)

        @block.tensor
        def _(pe):
            mm = nc.tensor.matmul
            def acquire(l, task):
                n, b, uses = at(l, task)
                if uses:
                    pe.wait_ge(bank_free[b], uses)

            def block_ready(l, n):
                pe.wait_ge(block_in[n % 2], 16 * (l * (NB // 2) + n // 2 + 1))

            def slot_of_block(n, k):
                return ring_w[:, n % 2, :].rearrange("p (k n) -> p k n", k=k)

            start = shorts = 0
            for l in range(L):
                for task in PLAN:
                    kind, i, j = task
                    if task == ("xt", 1, 0):
                        for t in range(TT):
                            for h in range(2):
                                n = BLOCK_OF["out", h]
                                if t == 0:
                                    block_ready(l, n)
                                for k in range(KD):
                                    if t == h == k % 2 == 0:
                                        pe.wait_ge(merged_ready, 4 * l + k // 2 + 1)
                                    ins = mm(acc[t][h][:], merged[:, k, P * t:P * t + P], slot_of_block(n, KD)[:, k, :],
                                             start=(k == 0), stop=(k == KD - 1))
                                ins.then_inc(h_ready, 1)
                    if kind == "rank":
                        n = BLOCK_OF["shared_down", 0]
                        block_ready(l, n)
                        wait_evac(pe, l, ("shared", 1, 0))
                        for t in range(TT):
                            for h in range(2):
                                for k in range(KF):
                                    ins = mm(acc[t][h][:], sh_t[:, k, P * t:P * t + P],
                                             ring_w[:, n % 2, D * k + 512 * h:D * k + 512 * h + 512],
                                             start=(k == 0), stop=(k == KF - 1))
                        ins.then_inc(shared_down, 1)
                    acquire(l, task)
                    b = bank(l, task)
                    if kind == "xt":
                        t = j // 2
                        if i == 0 and l == 0:
                            pe.wait_ge(x_in[t], 32 if t == 0 else 16)
                        else:
                            pe.wait_ge(ln_done, TT * (2 * l - 1 + i) + t + 1)
                        for c in range(4):
                            ins = nc.tensor.transpose(b[:, P * c:P * c + P], x_tok[:, t, 4 * (j % 2) + c::KD], ident)
                    elif kind == "z":
                        if i == 0:
                            for g in range(4):
                                wait_evac(pe, l, ("xt", 0, g))
                        n = CHUNK_AT["z", i // 2, i % 2]
                        pe.wait_ge(w_lo_ready, NC * l + n + 1)
                        hi, lo = chunk_part(w_hi, n), chunk_part(w_lo, n)
                        by_token = Z_BLOCKS[i // 2][0] in ("va", "vc")
                        for c in range(2):
                            cols = slice(P * c, P * c + P)
                            for k in range(KD):
                                for a, w in ((0, 0), (0, 1), (1, 0)):
                                    wk, xk = (hi, lo)[a][:, k, :], (x_hi, x_lo)[w][:, k, :]
                                    if by_token:
                                        lhs, rhs = (x_hi, x_lo)[a][:, k, cols], (hi, lo)[w][:, k, :]
                                    else:
                                        lhs, rhs = wk[:, cols], xk
                                    ins = mm(b[:, S * c:S * c + S], lhs, rhs, start=(k == 0 and a + w == 0),
                                             stop=(k == KD - 1 and a == 1))
                    elif kind == "scores":
                        branch, qt, g = unit(i)
                        W = P * (qt + 1)
                        if branch == 0 and i == 0 and j == 0:
                            for u in range(4):
                                wait_evac(pe, l, ("z", u, 0))
                        if branch == 1:
                            pe.wait_ge(rope_ready, 4 * (l + 1))
                        rows = slice(CHUNK * j, CHUNK * j + CHUNK)
                        for m in range(2):
                            ins = mm(b[:, W * m:W * m + W], q_t[branch][rows, 2 * g + m, P * qt:P * qt + P],
                                     k_t[branch][rows, 2 * g + m, 0:W], start=True, stop=True)
                    elif kind == "turn":
                        branch, qt, g = unit(i)
                        pe.wait_ge(probs_ready, l * UNITS + i + 1)
                        maps = (2 * j, 2 * j + 1) if branch == 0 else (0, 2)
                        for n, m in enumerate(maps):
                            for kt in range(qt + 1):
                                c = P * (n * (qt + 1) + kt)
                                ins = nc.tensor.transpose(b[:, c:c + P], probs[i % 2][:, m, P * kt:P * kt + P], ident)
                    elif kind == "pv":
                        branch, qt, g = unit(i)
                        for k in range(2 if branch == 0 else 1):
                            wait_evac(pe, l, ("turn", i, k))
                        if i in (0, 4):
                            first = 4 if branch == 0 else 10
                            wait_evac(pe, l, ("z", first, 0))
                            wait_evac(pe, l, ("z", first + 1, 0))
                        for m in range(4 if branch == 0 else 2):
                            for kt in range(qt + 1):
                                if branch == 0:
                                    o = b[CHUNK * (m % 2):CHUNK * (m % 2) + CHUNK, P * (m // 2):P * (m // 2) + P]
                                    val = va[:, kt, CHUNK * (4 * g + m):CHUNK * (4 * g + m) + CHUNK]
                                else:
                                    o = b[:, P * m:P * m + P]
                                    val = vc[:, kt, P * (2 * g + m):P * (2 * g + m) + P]
                                ins = mm(o, val, probs_t[:, m, kt, :], start=(kt == 0), stop=(kt == qt))
                    elif kind == "rope":
                        wait_evac(pe, l, ("z", (6, 8)[i] + j, 0))
                        if l == 0:
                            pe.wait_ge(const_in, 32)
                        for c in range(2):
                            ins = mm(b[:, S * c:S * c + S], const("rotate"), (qc_t, kc_t)[i][:, 2 * j + c, :],
                                     start=True, stop=True)
                    elif kind == "pool":
                        pe.wait_ge(mixed_ready, l + 1)
                        pe.wait_ge(params_in, 32 * (l + 1))
                        for c in range(2):
                            g = 2 * i + c
                            ins = mm(b[:, S * c:S * c + S], pool_w_sb[:, g, :], mixed[:, g, :], start=True, stop=True)
                    elif kind == "rms":
                        pe.wait_ge(squares_ready, l + 1)
                        for c in range(2):
                            ins = mm(b[:, S * c:S * c + S], const("ones"), squares[:, 2 * i + c, :], start=True, stop=True)
                    elif kind == "branch":
                        n = CHUNK_AT["branch", i, j // 2]
                        pe.wait_ge(w_lo_ready, NC * l + n + 1)
                        if j == 0:
                            if i == 0:
                                for k in range(4):
                                    wait_evac(pe, l, ("pv", k, 0))
                            else:
                                pe.wait_ge(y_lo_ready_of[i], l + 1)
                        w_parts = chunk_part(w_hi, n), chunk_part(w_lo, n)
                        for c in range(2):
                            cols = slice(P * (2 * (j % 2) + c), P * (2 * (j % 2) + c) + P)
                            for k in range(KW):
                                for a, w in ((0, 0), (0, 1), (1, 0)):
                                    ins = mm(b[:, S * c:S * c + S], w_parts[a][:, k, cols],
                                             (y_hi_of, y_lo_of)[w][i][:, k, :], start=(k == 0 and a + w == 0),
                                             stop=(k == KW - 1 and a == 1))
                    elif kind == "router":
                        for g in range(4):
                            wait_evac(pe, l, ("xt", 1, g))
                        for t in range(TT):
                            for k in range(KD):
                                ins = mm(b[:, NE * t:NE * t + NE], x_t[:, k, P * t:P * t + P], router_sb[:, k, :],
                                         start=(k == 0), stop=(k == KD - 1))
                    elif kind == "shared":
                        n = BLOCK_OF["shared_up", 0]
                        if i == 0:
                            block_ready(l, n)
                        for c in range(2):
                            col = FE * i + P * c
                            for k in range(KD):
                                ins = mm(b[:, S * c:S * c + S], slot_of_block(n, KD)[:, k, col:col + P], x_t[:, k, :],
                                         start=(k == 0), stop=(k == KD - 1))
                    elif kind == "rank":
                        pe.wait_ge(sel_ready, l + 1)
                        if l == 0:
                            pe.wait_ge(setup_done, 5)
                        mm(b[:, 0:NE], before_b[:], sel_b[:, 0, :], start=True, stop=True)
                        mm(b[:, NE:2 * NE], ones_b[:], sel_b[:, 0, :], start=True, stop=False)
                        mm(b[:, NE:2 * NE], before_b[:], sel_b[:, 1, :], start=False, stop=True)
                        mm(b[:, 2 * NE:3 * NE], ones_b[:], sel_b[:, 0, :], start=True, stop=False)
                        ins = mm(b[:, 2 * NE:3 * NE], ones_b[:], sel_b[:, 1, :], start=False, stop=True)
                    ins.then_inc(bank_ready, 1)

                def gather(n, half):
                    for c in range(4):
                        k = 4 * half + c
                        for t in range(TT):
                            for part in range(3):
                                ins = mm(bank_gather[:, P * c:P * c + P], parts[part][:, t, k, :], onehot[:, t, :],
                                         start=(t == 0 and part == 0), stop=(t == TT - 1 and part == 2))
                    ins.then_inc(gathered, 1)

                def combine(half, last=False):
                    for t in range(TT):
                        for part in (y_hi, y_lo):
                            ins = mm(acc[t][half][:], onehot_t[:, P * t:P * t + P], part[:, 512 * half:512 * half + 512],
                                     start=False, stop=True, skip_group_check=True)
                        if last:
                            ins.then_inc(acc_done, 1)
                    return ins

                def pair_step(n, first, odd, slot, loads):
                    bank_up, bank_other = (bank_even, bank_odd)[::-1 if odd else 1]
                    pe.wait_ge(sg_ready, n + l + 1)
                    if not first:
                        pe.wait_ge(onehot_t_ready, n)
                    for t in range(TT):
                        mm(bank_t[:, 0:1], gates[:, t, :], const("ones")[:, 0:1], start=(t == 0), stop=(t == TT - 1))
                    for t in range(TT):
                        ins = mm(bank_t[:, FE + P * t:FE + P * t + P], onehot[:, t, :], ident_b[:], start=True, stop=True)
                    ins.then_inc(slots_turned, 1)
                    pe.wait_ge(gu_in[slot], (32 if slot == 2 else 16) * loads)
                    if not first:
                        pe.wait_ge(y_ready, 2 * n - 1)
                    for k in range(KD):
                        if k % 4 == 0:
                            pe.wait_ge(xe_ready, 2 * (n + l) + k // 4 + 1)
                        for e in range(2):
                            ins = mm(bank_up[SLOTS * e:SLOTS * e + SLOTS, :], xe_t[:, k, SLOTS * e:SLOTS * e + SLOTS],
                                     gu[slot][:, e, k, :], start=(k == 0), stop=(k == KD - 1))
                    ins.then_inc(up_done, 1)
                    if not first:
                        pe.wait_ge(y_ready, 2 * n)
                        combine(0)
                    pe.wait_ge(hid_ready, n + 1)
                    for k in range(KF):
                        ins = nc.tensor.transpose(bank_t[:, P * k:P * k + P], hid[:, k::KF], ident)
                    ins.then_inc(hid_turned, 1)
                    if not first:
                        combine(1).then_inc(combined, 1)
                    pe.wait_ge(hid_t_ready, n + 1)
                    pe.wait_ge(dn_in[slot], 16 * loads)
                    for h in range(2):
                        for k in range(KF):
                            for e in range(2):
                                ins = mm((bank_other, bank_up)[h][SLOTS * e:SLOTS * e + SLOTS, :],
                                         hid_t[:, k, SLOTS * e:SLOTS * e + SLOTS],
                                         dn[slot][:, e, k, 512 * h:512 * h + 512], start=(k == 0), stop=(k == KF - 1))
                        ins.then_inc(y_done, 1)
                        if h == 0:
                            pe.wait_ge(s_ready, n + l + 2)
                        else:
                            pe.wait_ge(xe_ready, 2 * (n + 1 + l) + 1)
                        gather(n + 1, h)

                more = more_rounds(pe, l)
                for task in PLAN[-RING:]:
                    wait_evac(pe, l, task)
                pe.wait_ge(part_ready, 3 * TT * (l + 1))
                pe.wait_ge(s_ready, 2 * start + l + 1)
                gather(2 * start, 0)
                pe.wait_ge(xe_ready, 2 * (2 * start + l) + 1)
                gather(2 * start, 1)
                for n in range(2):
                    pair_step(2 * start + n, n == 0, n, n, loads_before(l, shorts, n) + 1)
                with pe.Fori(0, LONG) as i:
                    for u in range(SIX):
                        slot = (2 + u) % 3
                        pair_step(2 * start + SIX * i + 2 + u, False, u % 2, slot,
                                  loads_before(l, shorts, slot) + 2 * i + (2 + u) // 3 + 1)
                with pe.Fori(0, short_steps(more)) as i:
                    for u in range(2):
                        pair_step(2 * (i + start) + SHORT_FROM + u, False, u, u,
                                  loads_before(l, shorts, u) + i + IN_LONG + 1)
                shorts = shorts + short_steps(more)
                start = start + more * HALVES + HALVES
                pe.wait_ge(onehot_t_ready, 2 * start)
                pe.wait_ge(y_ready, 4 * start)
                combine(0, last=True)
                combine(1, last=True)
                pe.wait_ge(xe_ready, 2 * (2 * start + l) + 2)


def _constants():
    import numpy as np

    c = np.zeros((P, CONST_COLS), np.float32)

    def put(name, value):
        a, b = CONST[name]
        c[:, a:b] = value

    p = np.arange(P)
    half = ROPE_DIM // 2
    inv = np.float32(ROPE_THETA) ** (-np.arange(0, ROPE_DIM, 2, dtype=np.float32) / np.float32(ROPE_DIM))
    ang = np.arange(S, dtype=np.float32)[:, None] * inv[None, :].astype(np.float32)
    cos, sin = np.ones((P, S), np.float32), np.zeros((P, S), np.float32)
    rotate = np.zeros((P, P), np.float32)
    for base in (0, CHUNK):
        for n in range(half):
            for at in (base + n, base + half + n):
                cos[at], sin[at] = np.cos(ang[:, n]), np.sin(ang[:, n])
            rotate[base + half + n, base + n] = -1.0
            rotate[base + n, base + half + n] = 1.0
    put("cos", cos)
    put("sin", sin)
    put("rotate", rotate)
    put("ident", np.eye(P, dtype=np.float32))
    mask = np.zeros((P, S), np.float32)
    mask[:CHUNK, S - CHUNK:] = NEG
    put("mask", mask)
    put("iota", np.arange(SLOTS, dtype=np.float32)[None, :])
    g = np.arange(GROUPS)
    put("earlier", (g[None, :] < g[:, None]).astype(np.float32).reshape(1, -1))
    put("before", (p[:, None] < p[None, :]).astype(np.float32))
    put("ones", 1.0)
    t = np.arange(16)
    put("ramp", np.concatenate([w / np.minimum(t + 1, w) for w in POOL_WINDOWS]).astype(np.float32)[None, :])
    return c


_INS = ["x", "w_in", "rel_bias", "pool_w", "pool_scale", "lambda_q1", "lambda_k1", "lambda_q2", "lambda_k2",
        "subln_g", "w_branch_a", "w_branch_b", "w_branch_c", "w_out", "ln1_g", "ln1_b", "router_w", "router_bias",
        "expert_w_gate_up", "expert_w_down", "shared_w_gate_up", "shared_w_down", "ln2_g", "ln2_b"]


def kernel(**inputs):
    import numpy as _np
    import concourse.bacc as _bacc
    from concourse import mybir as _mybir
    from concourse.bass_utils import run_bass_kernel_spmd as _run

    nc = _bacc.Bacc("TRN2", target_bir_lowering=False, num_devices=1)
    arrays, args = {}, []
    for name in _INS:
        a = _np.ascontiguousarray(inputs[name])
        arrays[f"in_{name}"] = a
        args.append(nc.dram_tensor(f"in_{name}", a.shape, _mybir.dt.from_np(a.dtype), kind="ExternalInput").ap())
    table = _constants()
    arrays["in_consts"] = table
    args.append(nc.dram_tensor("in_consts", table.shape, _mybir.dt.from_np(table.dtype), kind="ExternalInput").ap())
    args.append([0.8 - 0.6 * float(_np.exp(-0.3 * l)) for l in range(L)])
    args.append(nc.dram_tensor("out_0", (1, S, D), _mybir.dt.float32, kind="ExternalOutput").ap())
    build(nc, *args)
    r = _run(nc, [arrays], core_ids=[0])
    return r.results[0]["out_0"]
```
